# Optimizing a Trainium2 kernel written in Bass

```python
import math
import jax
import jax.numpy as jnp
from jax import lax
import numpy as np

D_MODEL = 1024
BATCH = 1
SEQ = 256
DEPTH = 2

GRID_W = 64
CTX_LEN = 256
N_MOD = 9
D_FF = 2816
RMS_EPS = 1e-6
NEG_INF = -1e30
ROPE_THETA = 10000.0
N_MIX_GROUPS = 4
GROUP_W = D_MODEL // N_MIX_GROUPS
MIX_W = N_MIX_GROUPS * GROUP_W

MLA_HEADS = 4
MLA_NOPE = 64
MLA_ROPE = 32
MLA_V = GROUP_W // MLA_HEADS
MLA_Q_LORA = 256
MLA_KV_LORA = 128
MLA_QBLK = 128
NAT_HEADS = 4
NAT_HD = GROUP_W // NAT_HEADS
NAT_KR = 8
NAT_KC = 16
GDN_HEADS = 4
GDN_DK = 64
GDN_DV = GROUP_W // GDN_HEADS
GDN_CHUNK = 64
SSM_HEADS = 4
SSM_P = GROUP_W // SSM_HEADS
SSM_GROUPS = 2
SSM_STATE = 128
SSM_CHUNK = 128
CONV_K = 5

MLA_COLS = MLA_Q_LORA + MLA_KV_LORA + MLA_ROPE
NAT_COLS = 3 * GROUP_W
GDN_QK = GDN_HEADS * GDN_DK
GDN_QKV = 2 * GDN_QK + GDN_HEADS * GDN_DV
GDN_COLS = GDN_QKV + GROUP_W + 4 * GDN_HEADS
SSM_XBC = GROUP_W + 2 * SSM_GROUPS * SSM_STATE
SSM_COLS = GROUP_W + SSM_XBC + 2 * SSM_HEADS
IN_COLS = MLA_COLS + NAT_COLS + GDN_COLS + SSM_COLS

kernel_name = 'hybrid_parallel_group_diffusion_trunk'

def rms_norm(x, g):
    xf = x.astype(jnp.float32)
    y = xf * lax.rsqrt(jnp.mean(xf * xf, axis=-1, keepdims=True) + RMS_EPS)
    return (y * g.astype(jnp.float32)).astype(x.dtype)

def l2_norm(x):
    xf = x.astype(jnp.float32)
    return xf * lax.rsqrt(jnp.sum(xf * xf, axis=-1, keepdims=True) + RMS_EPS)

def modulate(x, g_pre, shift, scale):
    return rms_norm(x, g_pre) * (1.0 + scale) + shift

def swiglu(h, w1, w3, w2):
    return (jax.nn.silu(h @ w1) * (h @ w3)) @ w2

def half_ffn(v, shift, scale, gate, g_pre, g_post, w1, w3, w2):
    out = swiglu(modulate(v, g_pre, shift, scale), w1, w3, w2)
    return v + 0.5 * gate * rms_norm(out, g_post)

def flip_t(t):
    return jnp.flip(t, axis=1)

def centred_dwconv(x, w, b=None):
    y = lax.conv_general_dilated(
        x, w[:, None, :].astype(x.dtype), window_strides=(1,),
        padding=[(CONV_K // 2, CONV_K // 2)],
        dimension_numbers=('NWC', 'WIO', 'NWC'), feature_group_count=x.shape[-1])
    return y if b is None else y + b

def axial_rope(x, rows, cols):
    half = x.shape[-1] // 2
    quarter = half // 2
    freqs = ROPE_THETA ** (-jnp.arange(quarter, dtype=jnp.float32) / quarter)

    def rot(xa, pos):
        ang = pos[:, None] * freqs
        cos = jnp.cos(ang)[None, :, None, :]
        sin = jnp.sin(ang)[None, :, None, :]
        x1, x2 = xa[..., :quarter], xa[..., quarter:]
        return jnp.concatenate([x1 * cos - x2 * sin, x2 * cos + x1 * sin], axis=-1)

    out = jnp.concatenate([rot(x[..., :half], rows), rot(x[..., half:], cols)], axis=-1)
    return out.astype(x.dtype)

def mla_mixer(zl, zc, rows, cols, gq, gkv, wuq, wukv, gout, need_ctx):
    n_b, n_t = zl.shape[:2]
    dqk = MLA_NOPE + MLA_ROPE
    scale = dqk ** -0.5

    def project(z):
        t = z.shape[1]
        cq, ckv, k_rope = jnp.split(z, [MLA_Q_LORA, MLA_Q_LORA + MLA_KV_LORA], axis=-1)
        q = (rms_norm(cq, gq) @ wuq).reshape(n_b, t, MLA_HEADS, dqk)
        kv = (rms_norm(ckv, gkv) @ wukv).reshape(n_b, t, MLA_HEADS, MLA_NOPE + MLA_V)
        return q, kv[..., :MLA_NOPE], kv[..., MLA_NOPE:], k_rope[:, :, None, :]

    def keys(k_nope, k_rope):
        return jnp.concatenate(
            [k_nope, jnp.broadcast_to(k_rope, k_nope.shape[:-1] + (MLA_ROPE,))], axis=-1)

    q_l, kn_l, v_l, kr_l = project(zl)
    q_c, kn_c, v_c, kr_c = project(zc)
    q_l = jnp.concatenate([q_l[..., :MLA_NOPE], axial_rope(q_l[..., MLA_NOPE:], rows, cols)], axis=-1)
    k_l = keys(kn_l, axial_rope(kr_l, rows, cols))
    k_c = keys(kn_c, kr_c)

    n_blk = n_t // MLA_QBLK
    q_blocks = jnp.moveaxis(q_l.reshape(n_b, n_blk, MLA_QBLK, MLA_HEADS, dqk), 1, 0)

    def attend_block(qb):
        s = jnp.concatenate([jnp.einsum('bqhd,bkhd->bhqk', qb, k_l),
                             jnp.einsum('bqhd,bkhd->bhqk', qb, k_c)], axis=-1)
        p = jax.nn.softmax(s.astype(jnp.float32) * scale, axis=-1).astype(v_l.dtype)
        return (jnp.einsum('bhqk,bkhd->bqhd', p[..., :n_t], v_l)
                + jnp.einsum('bhqk,bkhd->bqhd', p[..., n_t:], v_c))

    o_l = jnp.moveaxis(lax.map(attend_block, q_blocks), 0, 1).reshape(n_b, n_t, GROUP_W)
    out_l = rms_norm(o_l, gout)
    out_c = None
    if need_ctx:
        s = jnp.einsum('bqhd,bkhd->bhqk', q_c, k_c).astype(jnp.float32) * scale
        p = jax.nn.softmax(s, axis=-1).astype(v_c.dtype)
        out_c = rms_norm(jnp.einsum('bhqk,bkhd->bqhd', p, v_c).reshape(n_b, -1, GROUP_W), gout)
    return out_l, out_c

def nat_mixer(zl, zc, rpb, gout, need_ctx):
    n_b, n_t = zl.shape[:2]
    n_rows = n_t // GRID_W
    kr = min(NAT_KR, n_rows)
    n_ctx = zc.shape[1]
    scale = NAT_HD ** -0.5
    ql, kl, vl = [t.reshape(n_b, n_rows, GRID_W, NAT_HEADS, NAT_HD) for t in jnp.split(zl, 3, axis=-1)]
    qc, kc, vc = [t.reshape(n_b, n_ctx, NAT_HEADS, NAT_HD) for t in jnp.split(zc, 3, axis=-1)]

    r = jnp.arange(n_rows)
    r0 = jnp.clip(r - kr // 2, 0, n_rows - kr)
    ridx = r0[:, None] + jnp.arange(kr)[None, :]
    cq = jnp.arange(GRID_W)
    c0 = jnp.clip(cq - NAT_KC // 2, 0, GRID_W - NAT_KC)
    cmask = (cq[None, :] >= c0[:, None]) & (cq[None, :] < c0[:, None] + NAT_KC)

    k_win = kl[:, ridx]
    v_win = vl[:, ridx]
    dr = ridx - r[:, None] + (NAT_KR - 1)
    dc = jnp.clip(cq[None, :] - cq[:, None] + (NAT_KC - 1), 0, 2 * NAT_KC - 2)
    bias = rpb[:, dr[:, None, :, None], dc[None, :, None, :]]
    bias = jnp.moveaxis(bias, 0, 1).astype(jnp.float32)

    s_win = jnp.einsum('brqhd,brjkhd->brhqjk', ql, k_win).astype(jnp.float32) * scale + bias
    s_win = jnp.where(cmask[:, None, :], s_win, NEG_INF)
    s_ctx = jnp.einsum('brqhd,bchd->brhqc', ql, kc).astype(jnp.float32) * scale
    n_win = kr * GRID_W
    s = jnp.concatenate([s_win.reshape(n_b, n_rows, NAT_HEADS, GRID_W, n_win), s_ctx], axis=-1)
    p = jax.nn.softmax(s, axis=-1).astype(vl.dtype)
    p_win = p[..., :n_win].reshape(n_b, n_rows, NAT_HEADS, GRID_W, kr, GRID_W)
    o = (jnp.einsum('brhqjk,brjkhd->brqhd', p_win, v_win)
         + jnp.einsum('brhqc,bchd->brqhd', p[..., n_win:], vc))
    out_l = rms_norm(o.reshape(n_b, n_t, GROUP_W), gout)
    out_c = None
    if need_ctx:
        sc = jnp.einsum('bqhd,bkhd->bhqk', qc, kc).astype(jnp.float32) * scale
        pc = jax.nn.softmax(sc, axis=-1).astype(vc.dtype)
        out_c = rms_norm(jnp.einsum('bhqk,bkhd->bqhd', pc, vc).reshape(n_b, n_ctx, GROUP_W), gout)
    return out_l, out_c

def gdn_chunked(q, k, v, g, beta, s0):
    n_b, n_t, n_h, _ = q.shape
    dv = v.shape[-1]
    cs = GDN_CHUNK
    n_c = n_t // cs

    def chunks(t):
        return jnp.moveaxis(t.reshape((n_b, n_c, cs) + t.shape[2:]), 3, 2)

    qc, kc, vc = chunks(q), chunks(k), chunks(v)
    gc = jnp.cumsum(chunks(g), axis=-1)
    bc = chunks(beta)
    incl = jnp.tril(jnp.ones((cs, cs), bool))
    strict = jnp.tril(jnp.ones((cs, cs), bool), -1)
    diff = gc[..., :, None] - gc[..., None, :]
    decay = jnp.where(incl, jnp.exp(jnp.where(incl, diff, 0.0)), 0.0)
    kb = kc * bc[..., None]
    lmat = jnp.where(strict, jnp.einsum('bnhid,bnhjd->bnhij', kb, kc) * decay, 0.0)
    rhs = jnp.concatenate([vc * bc[..., None], kb * jnp.exp(gc)[..., None]], axis=-1)
    sol = lax.linalg.triangular_solve(lmat, rhs, left_side=True, lower=True, unit_diagonal=True)
    u, w = sol[..., :dv], sol[..., dv:]
    a_intra = jnp.einsum('bnhid,bnhjd->bnhij', qc, kc) * decay
    q_dec = qc * jnp.exp(gc)[..., None]
    k_dec = kc * jnp.exp(gc[..., -1:] - gc)[..., None]
    g_last = jnp.exp(gc[..., -1])

    def step(s, inp):
        qd, kd, uu, ww, aa, gl = inp
        v_new = uu - jnp.einsum('bhck,bhkv->bhcv', ww, s)
        o = jnp.einsum('bhck,bhkv->bhcv', qd, s) + jnp.einsum('bhij,bhjv->bhiv', aa, v_new)
        s = s * gl[..., None, None] + jnp.einsum('bhck,bhcv->bhkv', kd, v_new)
        return s, o

    xs = tuple(jnp.moveaxis(t, 1, 0) for t in (q_dec, k_dec, u, w, a_intra, g_last))
    s_fin, o = lax.scan(step, s0, xs)
    o = jnp.moveaxis(jnp.moveaxis(o, 0, 1), 2, 3).reshape(n_b, n_t, n_h, dv)
    return o, s_fin

def gdn_mixer(zl, zc, conv_w, a_log, dt_bias, g_norm, need_ctx):
    f32 = jnp.float32
    n_b = zl.shape[0]

    def prep(z):
        n_t = z.shape[1]
        qkv, zg, b_raw, a_raw = jnp.split(
            z, [GDN_QKV, GDN_QKV + GROUP_W, GDN_QKV + GROUP_W + 2 * GDN_HEADS], axis=-1)
        qkv = jax.nn.silu(centred_dwconv(qkv, conv_w)).astype(f32)
        q, k, v = jnp.split(qkv, [GDN_QK, 2 * GDN_QK], axis=-1)
        q = l2_norm(q.reshape(n_b, n_t, GDN_HEADS, GDN_DK)) * (GDN_DK ** -0.5)
        k = l2_norm(k.reshape(n_b, n_t, GDN_HEADS, GDN_DK))
        v = v.reshape(n_b, n_t, GDN_HEADS, GDN_DV)
        beta = jax.nn.sigmoid(b_raw.astype(f32)).reshape(n_b, n_t, 2, GDN_HEADS)
        g = -jnp.exp(a_log.astype(f32)) * jax.nn.softplus(
            a_raw.astype(f32).reshape(n_b, n_t, 2, GDN_HEADS) + dt_bias.astype(f32))
        return q, k, v, beta, g, zg

    ql, kl, vl, bl, gl, zgl = prep(zl)
    qc, kc, vc, bc, gcx, zgc = prep(zc)
    s0 = jnp.zeros((n_b, GDN_HEADS, GDN_DK, GDN_DV), f32)
    oc_f, sc_f = gdn_chunked(qc, kc, vc, gcx[:, :, 0], bc[:, :, 0], s0)
    ol_f, _ = gdn_chunked(ql, kl, vl, gl[:, :, 0], bl[:, :, 0], sc_f)
    oc_b, sc_b = gdn_chunked(flip_t(qc), flip_t(kc), flip_t(vc), flip_t(gcx[:, :, 1]), flip_t(bc[:, :, 1]), s0)
    ol_b, _ = gdn_chunked(flip_t(ql), flip_t(kl), flip_t(vl), flip_t(gl[:, :, 1]), flip_t(bl[:, :, 1]), sc_b)

    def finish(o, zg):
        n_t = o.shape[1]
        gate = jax.nn.silu(zg.astype(f32)).reshape(n_b, n_t, GDN_HEADS, GDN_DV)
        return (rms_norm(o, g_norm) * gate).reshape(n_b, n_t, GROUP_W).astype(zg.dtype)

    out_l = finish(ol_f + flip_t(ol_b), zgl)
    out_c = finish(oc_f + flip_t(oc_b), zgc) if need_ctx else None
    return out_l, out_c

def ssd_chunked(x, dt, a, bm, cm, s0):
    n_b, n_t, n_h, n_p = x.shape
    cs = SSM_CHUNK
    n_c = n_t // cs
    xc = (x * dt[..., None]).reshape(n_b, n_c, cs, n_h, n_p)
    bc = bm.reshape(n_b, n_c, cs, n_h, SSM_STATE)
    cc = cm.reshape(n_b, n_c, cs, n_h, SSM_STATE)
    acum = jnp.cumsum(jnp.moveaxis((dt * a).reshape(n_b, n_c, cs, n_h), 3, 2), axis=-1)
    incl = jnp.tril(jnp.ones((cs, cs), bool))
    seg = jnp.where(incl, jnp.exp(jnp.where(incl, acum[..., :, None] - acum[..., None, :], 0.0)), 0.0)
    scores = jnp.einsum('bclhn,bcshn->bchls', cc, bc) * seg
    y_diag = jnp.einsum('bchls,bcshp->bclhp', scores, xc)
    decay_states = jnp.exp(acum[..., -1:] - acum)
    states = jnp.einsum('bclhn,bchl,bclhp->bchpn', bc, decay_states, xc)
    chunk_decay = jnp.exp(acum[..., -1])

    def step(s, inp):
        st, dec = inp
        return s * dec[..., None, None] + st, s

    s_fin, s_in = lax.scan(step, s0, (jnp.moveaxis(states, 1, 0), jnp.moveaxis(chunk_decay, 1, 0)))
    y_off = jnp.einsum('bclhn,bchpn,bchl->bclhp', cc, jnp.moveaxis(s_in, 0, 1), jnp.exp(acum))
    return (y_diag + y_off).reshape(n_b, n_t, n_h, n_p), s_fin

def ssm_mixer(zl, zc, conv_w, conv_b, a_log, dt_bias, d_skip, g_norm, need_ctx):
    f32 = jnp.float32
    n_b = zl.shape[0]
    rep = SSM_HEADS // SSM_GROUPS
    grp_w = GROUP_W // SSM_GROUPS

    def prep(z):
        n_t = z.shape[1]
        zg, xbc, dt_raw = jnp.split(z, [GROUP_W, GROUP_W + SSM_XBC], axis=-1)
        xbc = jax.nn.silu(centred_dwconv(xbc, conv_w, conv_b)).astype(f32)
        xs, bm, cm = jnp.split(xbc, [GROUP_W, GROUP_W + SSM_GROUPS * SSM_STATE], axis=-1)
        bm = jnp.repeat(bm.reshape(n_b, n_t, SSM_GROUPS, SSM_STATE), rep, axis=2)
        cm = jnp.repeat(cm.reshape(n_b, n_t, SSM_GROUPS, SSM_STATE), rep, axis=2)
        dt = jax.nn.softplus(dt_raw.astype(f32).reshape(n_b, n_t, 2, SSM_HEADS) + dt_bias.astype(f32))
        return xs.reshape(n_b, n_t, SSM_HEADS, SSM_P), bm, cm, dt, zg

    a = -jnp.exp(a_log.astype(f32))
    xl, bl, cl, dtl, zgl = prep(zl)
    xc, bc, cc, dtc, zgc = prep(zc)
    s0 = jnp.zeros((n_b, SSM_HEADS, SSM_P, SSM_STATE), f32)
    yc_f, sc_f = ssd_chunked(xc, dtc[:, :, 0], a[0], bc, cc, s0)
    yl_f, _ = ssd_chunked(xl, dtl[:, :, 0], a[0], bl, cl, sc_f)
    yc_b, sc_b = ssd_chunked(flip_t(xc), flip_t(dtc[:, :, 1]), a[1], flip_t(bc), flip_t(cc), s0)
    yl_b, _ = ssd_chunked(flip_t(xl), flip_t(dtl[:, :, 1]), a[1], flip_t(bl), flip_t(cl), sc_b)
    d = d_skip.astype(f32)[:, None]

    def finish(y, xs, zg):
        n_t = y.shape[1]
        y = (y + xs * d).reshape(n_b, n_t, GROUP_W) * jax.nn.silu(zg.astype(f32))
        y = rms_norm(y.reshape(n_b, n_t, SSM_GROUPS, grp_w), g_norm.reshape(SSM_GROUPS, grp_w))
        return y.reshape(n_b, n_t, GROUP_W).astype(zg.dtype)

    out_l = finish(yl_f + flip_t(yl_b), xl, zgl)
    out_c = finish(yc_f + flip_t(yc_b), xc, zgc) if need_ctx else None
    return out_l, out_c

def token_mixing(ul, uc, rows, cols, w_in, w_out, mla_gq, mla_gkv, mla_wuq, mla_wukv, mla_gout,
                 nat_rpb, nat_gout, gdn_conv_w, gdn_a_log, gdn_dt_bias, gdn_gnorm,
                 ssm_conv_w, ssm_conv_b, ssm_a_log, ssm_dt_bias, ssm_d, ssm_gnorm, need_ctx):
    bounds = [MLA_COLS, MLA_COLS + NAT_COLS, MLA_COLS + NAT_COLS + GDN_COLS]
    zla, zlb, zlc, zld = jnp.split(ul @ w_in, bounds, axis=-1)
    zca, zcb, zcc, zcd = jnp.split(uc @ w_in, bounds, axis=-1)
    a_l, a_c = mla_mixer(zla, zca, rows, cols, mla_gq, mla_gkv, mla_wuq, mla_wukv, mla_gout, need_ctx)
    b_l, b_c = nat_mixer(zlb, zcb, nat_rpb, nat_gout, need_ctx)
    c_l, c_c = gdn_mixer(zlc, zcc, gdn_conv_w, gdn_a_log, gdn_dt_bias, gdn_gnorm, need_ctx)
    d_l, d_c = ssm_mixer(zld, zcd, ssm_conv_w, ssm_conv_b, ssm_a_log, ssm_dt_bias, ssm_d, ssm_gnorm, need_ctx)
    y_lat = jnp.concatenate([a_l, b_l, c_l, d_l], axis=-1) @ w_out
    y_ctx = jnp.concatenate([a_c, b_c, c_c, d_c], axis=-1) @ w_out if need_ctx else None
    return y_lat, y_ctx

def setup_inputs(seed: int = 0) -> dict:
    key = jax.random.key(seed)
    ks = iter(jax.random.split(key, 48))
    f32 = jnp.float32
    dm, nl = D_MODEL, DEPTH

    def nrm(shape, scale):
        return jax.random.normal(next(ks), shape, f32) * scale

    def gain(shape):
        return 1.0 + nrm(shape, 0.02)

    def log_a(shape):
        return jnp.log(jax.random.uniform(next(ks), shape, f32, 1.0, 16.0))

    def dt_bias(shape):
        dt = jnp.exp(jax.random.uniform(next(ks), shape, f32, math.log(1e-3), math.log(1e-1)))
        return dt + jnp.log(-jnp.expm1(-dt))

    return {
        'x': nrm((BATCH, SEQ, dm), 1.0),
        'c': nrm((BATCH, dm), 1.0),
        'ctx': nrm((BATCH, CTX_LEN, dm), 1.0),
        'c_ctx': nrm((dm,), 1.0),
        'w_mod': nrm((nl, dm, N_MOD * dm), 0.5 * dm ** -0.5),
        'b_mod': nrm((nl, N_MOD * dm), 0.01),
        'norm_g': gain((nl, 6, dm)),
        'ffn1_w1': nrm((nl, dm, D_FF), dm ** -0.5),
        'ffn1_w3': nrm((nl, dm, D_FF), dm ** -0.5),
        'ffn1_w2': nrm((nl, D_FF, dm), D_FF ** -0.5),
        'ffn2_w1': nrm((nl, dm, D_FF), dm ** -0.5),
        'ffn2_w3': nrm((nl, dm, D_FF), dm ** -0.5),
        'ffn2_w2': nrm((nl, D_FF, dm), D_FF ** -0.5),
        'w_in': nrm((nl, dm, IN_COLS), dm ** -0.5),
        'w_out': nrm((nl, MIX_W, dm), MIX_W ** -0.5),
        'mla_gq': gain((nl, MLA_Q_LORA)),
        'mla_gkv': gain((nl, MLA_KV_LORA)),
        'mla_wuq': nrm((nl, MLA_Q_LORA, MLA_HEADS * (MLA_NOPE + MLA_ROPE)), MLA_Q_LORA ** -0.5),
        'mla_wukv': nrm((nl, MLA_KV_LORA, MLA_HEADS * (MLA_NOPE + MLA_V)), MLA_KV_LORA ** -0.5),
        'mla_gout': gain((nl, GROUP_W)),
        'nat_rpb': nrm((nl, NAT_HEADS, 2 * NAT_KR - 1, 2 * NAT_KC - 1), 0.05),
        'nat_gout': gain((nl, GROUP_W)),
        'gdn_conv_w': nrm((nl, CONV_K, GDN_QKV), CONV_K ** -0.5),
        'gdn_a_log': log_a((nl, 2, GDN_HEADS)),
        'gdn_dt_bias': dt_bias((nl, 2, GDN_HEADS)),
        'gdn_gnorm': gain((nl, GDN_DV)),
        'ssm_conv_w': nrm((nl, CONV_K, SSM_XBC), CONV_K ** -0.5),
        'ssm_conv_b': nrm((nl, SSM_XBC), 0.01),
        'ssm_a_log': log_a((nl, 2, SSM_HEADS)),
        'ssm_dt_bias': dt_bias((nl, 2, SSM_HEADS)),
        'ssm_d': 1.0 + nrm((nl, SSM_HEADS), 0.1),
        'ssm_gnorm': gain((nl, GROUP_W)),
    }

def reference(x, c, ctx, c_ctx, w_mod, b_mod, norm_g, ffn1_w1, ffn1_w3, ffn1_w2,
              ffn2_w1, ffn2_w3, ffn2_w2, w_in, w_out, mla_gq, mla_gkv, mla_wuq, mla_wukv,
              mla_gout, nat_rpb, nat_gout, gdn_conv_w, gdn_a_log, gdn_dt_bias, gdn_gnorm,
              ssm_conv_w, ssm_conv_b, ssm_a_log, ssm_dt_bias, ssm_d, ssm_gnorm):
    n_b, n_tok, _ = x.shape
    pos = jnp.arange(n_tok)
    rows = (pos // GRID_W).astype(jnp.float32)
    cols = (pos % GRID_W).astype(jnp.float32)
    sc = jax.nn.silu(c)
    scc = jax.nn.silu(c_ctx)
    h, hc = x, ctx
    for l in range(DEPTH):
        need_ctx = l < DEPTH - 1
        m_lat = (sc @ w_mod[l] + b_mod[l]).reshape(n_b, N_MOD, 1, D_MODEL)
        m_ctx = (scc @ w_mod[l] + b_mod[l]).reshape(N_MOD, 1, D_MODEL)
        ml = [m_lat[:, i] for i in range(N_MOD)]
        mc = [m_ctx[i] for i in range(N_MOD)]
        g = norm_g[l]
        h = half_ffn(h, ml[0], ml[1], ml[2], g[0], g[1], ffn1_w1[l], ffn1_w3[l], ffn1_w2[l])
        hc = half_ffn(hc, mc[0], mc[1], mc[2], g[0], g[1], ffn1_w1[l], ffn1_w3[l], ffn1_w2[l])
        ul = modulate(h, g[2], ml[3], ml[4])
        uc = modulate(hc, g[2], mc[3], mc[4])
        y_lat, y_ctx = token_mixing(
            ul, uc, rows, cols, w_in[l], w_out[l], mla_gq[l], mla_gkv[l], mla_wuq[l], mla_wukv[l],
            mla_gout[l], nat_rpb[l], nat_gout[l], gdn_conv_w[l], gdn_a_log[l], gdn_dt_bias[l],
            gdn_gnorm[l], ssm_conv_w[l], ssm_conv_b[l], ssm_a_log[l], ssm_dt_bias[l], ssm_d[l],
            ssm_gnorm[l], need_ctx)
        h = h + ml[5] * rms_norm(y_lat, g[3])
        h = half_ffn(h, ml[6], ml[7], ml[8], g[4], g[5], ffn2_w1[l], ffn2_w3[l], ffn2_w2[l])
        if need_ctx:
            hc = hc + mc[5] * rms_norm(y_ctx, g[3])
            hc = half_ffn(hc, mc[6], mc[7], mc[8], g[4], g[5], ffn2_w1[l], ffn2_w3[l], ffn2_w2[l])
    return h


_drawn_inputs = setup_inputs


def setup_inputs(seed=0):
    import zlib

    import numpy as np

    out = dict(_drawn_inputs(seed))
    spreads = {}
    factors = {'norm_g': 3.527,
     'mla_gq': 8.0,
     'mla_gkv': 8.0,
     'mla_gout': 35.699,
     'nat_rpb': 8.0,
     'nat_gout': 34.141,
     'gdn_a_log': 3.975,
     'gdn_gnorm': 8.0,
     'ssm_conv_b': 26.967,
     'ssm_d': 64.0,
     'ssm_gnorm': 34.381}
    for name, (base, spread) in spreads.items():
        noise = np.random.default_rng([zlib.crc32(name.encode()), seed]).standard_normal(out[name].shape)
        drawn = base * np.exp(spread * noise) if base else spread * noise
        out[name] = jnp.asarray(drawn.astype(out[name].dtype))
    for name, factor in factors.items():
        out[name] = (out[name] * factor).astype(out[name].dtype)
    return out
```

```python
from contextlib import ExitStack

import numpy as np

import concourse.bass as bass
from concourse import mybir

F32 = mybir.dt.float32
ALU = mybir.AluOpType
ACT = mybir.ActivationFunctionType
AX = mybir.AxisListType.X

P = 128
RING = 3
SLOT = 8 * 528
EPS = 1e-6
NEG = -1e30

N_LEVELS = 7
C_IDENT, C_ONES, C_TRI, C_NEG, C_HALF, C_NATM = 0, 128, 256, 512, 768, 896
C_COS, C_SIN, C_ROT, C_SEL, C_LEV = 960, 1216, 1472, 1504, 1506
C_FLIP = C_LEV + 2 * N_LEVELS * P
C_END = C_FLIP + P


def constants(grid_w, window, theta, rope, lat):
    c = np.zeros((P, C_END), np.float32)
    j, i = np.arange(P)[:, None], np.arange(P)[None, :]
    c[:, C_IDENT:C_IDENT + P] = j == i
    c[:, C_ONES:C_ONES + P] = 1.0
    for d, keep in enumerate((j <= i, j >= i)):
        c[:, C_TRI + d * P:C_TRI + (d + 1) * P] = keep
        c[:, C_NEG + d * P:C_NEG + (d + 1) * P] = np.where(keep, 0.0, NEG)
    c[:, C_SEL:C_SEL + 2] = (j // 64) == np.arange(2)[None, :]
    c[:, C_FLIP:C_FLIP + P] = (j // grid_w == i // grid_w) & (j % grid_w == grid_w - 1 - i % grid_w)
    q, k = grid_w - 1 - np.arange(P)[:, None] % grid_w, np.arange(grid_w)[None, :]
    first = np.clip(q - window // 2, 0, grid_w - window)
    c[:, C_NATM:C_NATM + grid_w] = np.where((k >= first) & (k < first + window), 0.0, NEG)
    quarter = rope // 4
    freqs = theta ** (-np.arange(quarter, dtype=np.float32) / quarter)
    pos = np.arange(lat)
    for h, p in enumerate((pos // grid_w, pos % grid_w)):
        ang = (p[None, :].astype(np.float32) * freqs[:, None]).astype(np.float32)
        for r in range(2):
            at = 64 + h * 2 * quarter + r * quarter
            c[at:at + quarter, C_COS:C_COS + lat] = np.cos(ang)
            c[at:at + quarter, C_SIN:C_SIN + lat] = np.sin(ang)
        for n in range(quarter):
            a, b = h * 2 * quarter + n, h * 2 * quarter + quarter + n
            c[64 + b, C_ROT + a] = -1.0
            c[64 + a, C_ROT + b] = 1.0
    for d in range(2):
        for s in range(N_LEVELS):
            size = 1 << s
            same = (j // (2 * size)) == (i // (2 * size))
            lo, hi = (j // size) % 2 == 0, (i // size) % 2 == 1
            m = same & (lo & hi if d == 0 else ~lo & ~hi)
            at = C_LEV + (d * N_LEVELS + s) * P
            c[:, at:at + P] = m
    return c


def trunk(nc, out, consts, x, c, ctx, c_ctx, w_mod, b_mod, norm_g, ffn1_w1, ffn1_w3, ffn1_w2,
          ffn2_w1, ffn2_w3, ffn2_w2, w_in, w_out, mla_gq, mla_gkv, mla_wuq, mla_wukv, mla_gout, nat_rpb,
          nat_gout, gdn_conv_w, gdn_a_log, gdn_dt_bias, gdn_gnorm, ssm_conv_w, ssm_conv_b, ssm_a_log,
          ssm_dt_bias, ssm_d, ssm_gnorm):
    LAYERS, D, _ = w_in.shape
    KC = D // P
    FF = ffn1_w1.shape[2]
    FB = FF // P
    LAT, CTX = x.shape[1], ctx.shape[1]
    T = LAT + CTX
    HALF = CTX
    assert LAT == CTX == 256 and D == 1024 and FF == 2816
    NMOD = w_mod.shape[2] // D
    NH = 4
    ROWS, RW = 4, 64
    NT = T // P
    MLA_SCALE, NAT_SCALE, GDN_SCALE = 96 ** -0.5, 64 ** -0.5, 64 ** -0.5

    MOD_PIECES = NMOD * D // 512
    UP_PIECES = FF // 256
    DOWN_PIECES = KC
    IN_PIECES = [(1184, 512), (1696, 528), (2224, 512), (2736, 520), (0, 416), (416, 512), (928, 256)]
    OUT_PIECES = 2
    stages = []
    for l in range(LAYERS):
        stages += [("mod", l, MOD_PIECES), ("up0", l, UP_PIECES), ("down0", l, DOWN_PIECES),
                   ("in", l, len(IN_PIECES)), ("out", l, OUT_PIECES),
                   ("up1", l, UP_PIECES), ("down1", l, DOWN_PIECES)]
    FIRST_PIECE, n = {}, 0
    for name, l, count in stages:
        FIRST_PIECE[name, l] = n
        n += count

    es = ExitStack()
    with es:
        def sb(name, shape):
            return es.enter_context(nc.sbuf_tensor(name, shape, F32))

        cst = sb("cst", [P, C_END])
        xT = sb("xT", [P, KC, T])
        uT = sb("uT", [P, KC, T])
        ring = sb("ring", [P, RING, SLOT])
        arena = sb("arena", [P, 25696])
        prm = sb("prm", [P, LAYERS, 196])
        gpar = sb("gpar", [P, LAYERS, 36])
        modT = sb("modT", [P, NMOD * KC, 2])
        gpre = sb("gpre", [P, 3, KC, 2])
        gpost = sb("gpost", [P, 3, KC, 2])
        scT = sb("scT", [P, KC, 2])
        epsc = sb("epsc", [P, 2])
        std = sb("std", [P, 64])
        rst = sb("rst", [P, 64])
        gates = sb("gates", [P, 12, NT, 16])
        small = sb("small", [P, 64])
        mlaw = sb("mlaw", [P, 2 * 384 + 512])

        ps = [es.enter_context(nc.psum_tensor(f"bank{b}", [P, 512], F32)) for b in range(8)]

        sems = {}

        def sem(name):
            if name not in sems:
                sems[name] = es.enter_context(nc.semaphore(name))
            return sems[name]

        ident = cst[:, C_IDENT:C_IDENT + P]
        ones = cst[:, C_ONES:C_ONES + P]
        flip = cst[:, C_FLIP:C_FLIP + P]

        def tri(d):
            return cst[:, C_TRI + d * P:C_TRI + (d + 1) * P]

        def negmask(d):
            return cst[:, C_NEG + d * P:C_NEG + (d + 1) * P]

        def view(at, *shape, parts=slice(0, P)):
            n = int(np.prod(shape))
            v = arena[parts, at:at + n]
            if len(shape) == 1:
                return v
            names = "abcd"[:len(shape)]
            return v.rearrange(f"p ({' '.join(names)}) -> p {' '.join(names)}",
                               **{k: s for k, s in zip(names, shape)})

        hT = view(0, FB, T)
        sq = view(FB * T, KC, T)
        FT = FB * T + KC * T
        silu_t = view(FT, 2, T)
        ysq = view(FT + 1024, T)
        yacc = view(FT + 1536, T)
        convT = view(0, 12, T)
        zgG = view(6144, NT, 272)
        zgS = view(7232, NT, 256)
        dtr = view(8256, NT, 8)
        cT = view(8288, 3, T)
        krT = view(9824, T)
        nqkT = view(10336, 4, T)
        natv = view(12384, NT, 256)
        cin = view(13408, 12, 2, 260)
        ATT = 13408
        mqT = view(ATT, NH, T)
        mkT = view(ATT + 2048, NH, T)
        mlav = view(ATT + 4096, NT, 256)
        prob = view(ATT + 5120, 2, T)
        probT = view(ATT + 6144, 2, T)
        csq = view(ATT + 5120, 3, T)
        rope_t = view(ATT + 5120, NH, LAT)
        att_o = view(ATT + 7168, 2, NT, 256)
        natb = view(ATT + 9216, 2, NH, 256)
        att_sq = view(ATT, 2, NT, 256)
        k_tm = view(8288, NT, 256)
        v_tm = view(9312, NT, 256)
        x_tm = view(10336, NT, 256)
        b_tm = view(11360, NT, 256)
        AT = view(12384, 2, NT, NH * P)
        UT = view(16480, 2, NT, NH * P)
        dec = view(20576, 2, NH * P)
        LT = view(21600, 2, NH * P)
        Tm = view(22624, 2, NH * P)
        P1 = view(23648, 2, NH * P)
        XT = view(24672, 2, NH * P)
        qksq = view(12384, 4, T)
        o_tm = view(2048, NT, 256)
        y_tm = view(3072, NT, 256)
        sdec = dec
        S_g = view(21600, 4, P)
        r_g = view(22112, 2, 256)
        vn_g = view(22624, 2, 256)
        kd_g = view(23136, 2, 256)
        tmp_g = view(23648, 2, 256)
        S_s = view(24160, 2, 256)
        tmp_s = view(24672, 2, 256)
        sc_s = uT[:, 4:6, :]
        xdt = uT[:, 6, :].rearrange("p (d n) -> p d n", d=2)
        xdc = uT[:, 7, :].rearrange("p (d n) -> p d n", d=2)
        fin_sq = view(20576, 2, NT, 256)
        xin = view(0, NT, D)
        prow = view(4096, LAYERS, 2, P)
        crow = view(4608, P)
        uTf = uT[:, :, :].rearrange("p k t -> p (k t)")

        PARAM_DMAS = 7 + LAYERS * 17

        def rows(w):
            return w.rearrange("(k p) n -> p k n", p=P)

        weights_landed = [sem(f"weights_landed{s}") for s in range(RING)]
        met = sem("met")

        def landed(eng, n0, j, turns=0):
            eng.wait_ge(weights_landed[(n0 + j) % RING], 32 * ((n0 + j) // RING + 1) + 32 * turns)

        def over_pieces(eng, count, body):
            with eng.Fori(0, count // RING) as turn:
                for j in range(RING):
                    body(turn, j)
            for j in range(count % RING):
                body(count // RING, j)

        def meeting(eng):
            count = [0]

            def meet():
                count[0] += 1
                eng.drain().then_inc(met, 1)
                eng.wait_ge(met, 4 * count[0])
            return meet

        def linked(eng, s):
            count = [0]

            def link(ins):
                count[0] += 1
                ins.then_inc(s, 1)
                eng.wait_ge(s, count[0])
            return link

        pieces_done = sem("pieces_done")
        params_in, mla_w_in, nat_bias_in = sem("params_in"), sem("mla_w_in"), sem("nat_bias_in")
        setup_t, setup_copied = sem("setup_t"), sem("setup_copied")
        mod_ready = sem("mod_ready")
        x_ready, x_squared, x_scaled = sem("x_ready"), sem("x_squared"), sem("x_scaled")
        u_dve, u_act = sem("u_dve"), sem("u_act")
        sums_ready, rms_ready, rstd_ready, rms_spread = (
            sem("sums_ready"), sem("rms_ready"), sem("rstd_ready"), sem("rms_spread"))
        even_up, silu_done, gated = sem("even_up"), sem("silu_done"), sem("gated")
        y_mixed, y_copied, y_sq, y_summed, y_scaled = (
            sem("y_mixed"), sem("y_copied"), sem("y_sq"), sem("y_summed"), sem("y_scaled"))
        proj_ready, proj_copied, pads_zero, conv_done, conv_act = (
            sem("proj_ready"), sem("proj_copied"), sem("pads_zero"), sem("conv_done"), sem("conv_act"))

        UNITS = []
        for b in range(4):
            UNITS.append(("fm", 0, b * P, P, ("cin", b)))
        for b in range(2):
            UNITS.append(("fm", 1, b * P, P, ("cin", 4 + b)))
        UNITS += [(t, 1, 256, 272, ("zgG", t)) for t in range(NT)]
        UNITS += [(t, 2, 0, 256, ("zgS", t)) for t in range(NT)]
        for b in range(2):
            UNITS.append(("fm", 2, 256 + b * P, P, ("cin", 6 + b)))
        for b in range(4):
            UNITS.append(("fm", 3, b * P, P, ("cin", 8 + b)))
        UNITS += [(t, 3, 512, 8, ("dtr", t)) for t in range(NT)]
        for b in range(3):
            UNITS.append(("fm", 4, b * P, P, ("cT", b)))
        UNITS.append(("fm", 4, 384, 32, ("krT", 0)))
        for b in range(4):
            UNITS.append(("fm", 5, b * P, P, ("nqkT", b)))
        UNITS += [(t, 6, 0, 256, ("natv", t)) for t in range(NT)]
        NU = len(UNITS)
        CIN_UNIT = {d[1]: n for n, (_, _, _, _, d) in enumerate(UNITS) if d[0] == "cin"}
        B_TILE = (1, 0, 3, 2)

        def tile_of(d, n):
            return n if d == 0 else B_TILE[n]

        def att_units(l):
            tiles = range(NT) if l < LAYERS - 1 else (2, 3)
            return [(mx, t, h) for mx in range(2) for t in tiles for h in range(NH)]

        ATT_BEFORE = [sum(len(att_units(i)) for i in range(l)) for l in range(LAYERS + 1)]
        NLV = N_LEVELS - 1
        Y_BANKS = (4, 5, 7)
        Y_CREDIT, GATE_CREDIT = 3, 2

        def halves(l, after):
            return (0, 1) if l < LAYERS - 1 or not after else (1,)

        def tiles_of(hs):
            return [2 * h + i for h in hs for i in range(2)]

        SUBS = ((0, False), (1, True), (2, True))

        block = es.enter_context(nc.Block())

        @block.sync
        def _(sp):
            def piece(n, turn, srcs):
                if n >= RING:
                    sp.wait_ge(pieces_done, n - RING + 1 + RING * turn)
                for dst, src in srcs:
                    sp.dma_start(dst, src).then_inc(weights_landed[n % RING], 16)

            def cols(n, k, w):
                return ring[:, n % RING, 0:k * w].rearrange("p (k w) -> p k w", k=k)

            def stage(n0, count, srcs):
                whole = count // RING
                if n0 == 0:
                    for j in range(RING):
                        piece(j, 0, srcs(j, j))
                    with sp.Fori(0, whole - 1) as turn:
                        for j in range(RING):
                            piece(RING + j, turn, srcs(turn * RING + RING + j, j))
                else:
                    with sp.Fori(0, whole) as turn:
                        for j in range(RING):
                            piece(n0 + j, turn, srcs(turn * RING + j, n0 + j))
                for j in range(count % RING):
                    piece(n0 + whole * RING + j, 0, srcs(whole * RING + j, n0 + whole * RING + j))

            def mod_srcs(wm):
                def srcs(p, n):
                    dst = cols(n, KC, 512)
                    return [(dst[:, h:h + 4, :], wm[:, h:h + 4, bass.ds(p * 512, 512)]) for h in (0, 4)]
                return srcs

            def up_srcs(w1, w3):
                def srcs(p, n):
                    dst = ring[:, n % RING, 0:4096].rearrange("p (w k n) -> p w k n", w=2, k=KC)
                    return [(dst[:, i], w[:, :, bass.ds(p * 256, 256)]) for i, w in enumerate((w1, w3))]
                return srcs

            def down_srcs(w2):
                def srcs(p, n):
                    dst = cols(n, FB, P)
                    return [(dst[:, h:h + 11, :], w2[:, h:h + 11, bass.ds(p * P, P)]) for h in (0, 11)]
                return srcs

            sp.dma_start(cst[:, :], consts[:, :]).then_inc(params_in, 16)
            for t in range(NT):
                src = (ctx if t < 2 else x)[0, (t % 2) * P:(t % 2 + 1) * P, :]
                sp.dma_start(xin[:, t, :], src).then_inc(params_in, 16)
            sp.dma_start(crow[0:8, :], c_ctx.rearrange("(k p) -> k p", p=P)).then_inc(params_in, 16)
            sp.dma_start(crow[8:16, :], c[0].rearrange("(k p) -> k p", p=P)).then_inc(params_in, 16)
            dmas = 7
            for l in range(LAYERS):
                a, b = prow[:, l, 0, :], prow[:, l, 1, :]
                rows_of = [(a[0:72], b_mod[l].rearrange("(m p) -> m p", p=P)),
                           (a[72:120], norm_g[l].rearrange("j (m p) -> (j m) p", p=P)),
                           (b[0:30], gdn_conv_w[l].rearrange("k (m p) -> (k m) p", p=P)),
                           (b[30:60], ssm_conv_w[l].rearrange("k (m p) -> (k m) p", p=P)),
                           (b[60:66], ssm_conv_b[l].rearrange("(m p) -> m p", p=P)),
                           (b[66:68], mla_gq[l].rearrange("(m p) -> m p", p=P)),
                           (b[68:69], mla_gkv[l].rearrange("(m p) -> m p", p=P)),
                           (b[69:71], mla_gout[l].rearrange("(m p) -> m p", p=P)),
                           (b[71:73], nat_gout[l].rearrange("(m p) -> m p", p=P)),
                           (b[73:75], ssm_gnorm[l].rearrange("(m p) -> m p", p=P)),
                           (b[75:76, 0:64], gdn_gnorm[l].rearrange("(m p) -> m p", p=64)),
                           (b[75:76, 64:128], gdn_gnorm[l].rearrange("(m p) -> m p", p=64))]
                for at, gp, sp_ in ((0, gdn_dt_bias, ssm_dt_bias), (16, gdn_a_log, ssm_a_log)):
                    for kind, par in enumerate((gp, sp_)):
                        dst = gpar[:, l, at:at + 16].rearrange("p (d k h) -> p d k h", d=2, k=2)[:, :, kind, :]
                        rows_of.append((dst, par[l].partition_broadcast(P)))
                rows_of.append((gpar[:, l, 32:36], ssm_d[l].partition_broadcast(P)))
                for dst, src in rows_of:
                    sp.dma_start(dst, src).then_inc(params_in, 16)
                dmas += len(rows_of)
            assert dmas == PARAM_DMAS
            for l in range(LAYERS):
                stage(FIRST_PIECE["mod", l], MOD_PIECES, mod_srcs(rows(w_mod[l])))
                stage(FIRST_PIECE["up0", l], UP_PIECES, up_srcs(rows(ffn1_w1[l]), rows(ffn1_w3[l])))
                stage(FIRST_PIECE["down0", l], DOWN_PIECES, down_srcs(rows(ffn1_w2[l])))
                sp.dma_start(mlaw[:, 0:768].rearrange("p (k n) -> p k n", k=2), rows(mla_wuq[l])
                             ).then_inc(mla_w_in, 16)
                sp.dma_start(mlaw[:, 768:1280], mla_wukv[l]).then_inc(mla_w_in, 16)
                with nc.allow_non_contiguous_dma(reason="Toeplitz expansion of the window bias"):
                    for t in range(2):
                        for rq in range(2):
                            for h in range(NH):
                                at = ((l * NH + h) * 15 + 7 - (2 * t + rq)) * 31 + 15 - (RW - 1)
                                src = bass.AP(nat_rpb.tensor, at, [(1, RW), (31, ROWS), (1, RW)])
                                dst = natb[rq * RW:(rq + 1) * RW, t, h, :].rearrange("p (r k) -> p r k", r=ROWS)
                                sp.dma_start(dst, src).then_inc(nat_bias_in, 16)
                wi, wo = rows(w_in[l]), rows(w_out[l])
                for j, (c0, w) in enumerate(IN_PIECES):
                    n = FIRST_PIECE["in", l] + j
                    dst = cols(n, KC, w)
                    piece(n, 0, [(dst[:, h:h + 4, :], wi[:, h:h + 4, c0:c0 + w]) for h in (0, 4)])
                for j in range(OUT_PIECES):
                    n = FIRST_PIECE["out", l] + j
                    dst = cols(n, KC, 512)
                    piece(n, 0, [(dst[:, h:h + 4, :], wo[:, h:h + 4, j * 512:(j + 1) * 512]) for h in (0, 4)])
                stage(FIRST_PIECE["up1", l], UP_PIECES, up_srcs(rows(ffn2_w1[l]), rows(ffn2_w3[l])))
                stage(FIRST_PIECE["down1", l], DOWN_PIECES, down_srcs(rows(ffn2_w2[l])))
            sp.wait_ge(sem("out_copied"), 4)
            sp.dma_start(out.rearrange("b (t p) n -> p (b t) n", p=P), view(0, 2, D)).then_inc(sem("stored"), 16)
            sp.wait_ge(sem("stored"), 16)

        @block.tensor
        def _(pe):
            meet = meeting(pe)

            def landed(n, turn=0):
                pe.wait_ge(weights_landed[n % RING], 32 * (n // RING + 1) + 32 * turn)

            def setup():
                pe.wait_ge(params_in, 16 * PARAM_DMAS)
                for l in range(LAYERS):
                    for r, (at, n) in enumerate(((0, 120), (120, 76))):
                        last = pe.transpose(ps[0][:, l * 196 + at:l * 196 + at + n], prow[0:n, l, r, :],
                                            ident[0:n, 0:n])
                last.then_inc(setup_t, 1)
                pe.transpose(ps[1][:, 0:16], crow[0:16, :], ident[0:16, 0:16]).then_inc(setup_t, 1)
                for m in range(KC):
                    if m >= 6:
                        pe.wait_ge(setup_copied, m - 5)
                    for t in range(NT):
                        last = pe.transpose(ps[(2 + m) % 8][:, t * P:(t + 1) * P],
                                            xin[:, t, m * P:(m + 1) * P], ident)
                    last.then_inc(setup_t, 1)

            def mod(l):
                n0 = FIRST_PIECE["mod", l]

                def body(turn, j):
                    landed(n0 + j, turn)
                    w = ring[:, (n0 + j) % RING, 0:4096].rearrange("p (k n) -> p k n", k=KC)
                    for b in range(4):
                        for k in range(KC):
                            last = pe.matmul(ps[7][:, bass.ds(turn * (RING * 8) + (j * 4 + b) * 2, 2)],
                                             w[:, k, b * P:(b + 1) * P], scT[:, k, :],
                                             start=k == 0, stop=k == KC - 1)
                    last.then_inc(pieces_done, 1)
                over_pieces(pe, MOD_PIECES, body)

            def norm(n, src, blocks, tiles):
                for t in tiles:
                    for m in range(blocks):
                        last = pe.matmul(ps[6][:, t:t + 1], src(m)[:, t * P:(t + 1) * P], ones[:, 0:1],
                                         start=m == 0, stop=m == blocks - 1)
                last.then_inc(sums_ready, 1)
                pe.wait_ge(rstd_ready, n + 1)
                for t in tiles:
                    last = pe.matmul(ps[5][:, t * P:(t + 1) * P], rst[:, t:t + 1].to_broadcast([P, P]),
                                     ident, start=True, stop=True)
                last.then_inc(rms_spread, 1)

            def prenorm(l, j, hs):
                pe.wait_ge(x_squared, 8 * (3 * l + j + 1))
                norm(6 * l + 2 * j, lambda m: sq[:, m, :], KC, tiles_of(hs))

            def postnorm(l, j, hs):
                pe.wait_ge(y_summed, 9 * (3 * l + j + 1))
                norm(6 * l + 2 * j + 1, lambda m: yacc, 1, tiles_of(hs))

            def input_ready(l, j, hs):
                pe.wait_ge(u_dve, 8 * (3 * l + j + 1))
                if 0 in hs:
                    pe.wait_ge(u_act, 8 * (3 * l + j + 1))

            def ffn(l, f, hs):
                t0 = HALF * hs[0]
                u, d = FIRST_PIECE[f"up{f}", l], FIRST_PIECE[f"down{f}", l]
                i, q = 2 * l + f, 3 * l + 2 * f
                input_ready(l, 2 * f, hs)

                def up(turn, j):
                    landed(u + j, turn)
                    w = ring[:, (u + j) % RING, 0:4096].rearrange("p (w k n) -> p w k n", w=2, k=KC)
                    for b in range(2):
                        pe.wait_ge(gated, FB * i + 2 * j + b - 1 + GATE_CREDIT + turn * (2 * RING))
                        for g in range(2):
                            for k in range(KC):
                                last = pe.matmul(ps[2 * b + g][:, t0:T], w[:, g, k, b * P:(b + 1) * P],
                                                 uT[:, k, t0:T], start=k == 0, stop=k == KC - 1)
                        last.then_inc(even_up if b == 0 else pieces_done, 1)
                over_pieces(pe, UP_PIECES, up)
                pe.wait_ge(gated, GATE_CREDIT + FB * (i + 1))

                def down(turn, j):
                    landed(d + j, turn)
                    w = ring[:, (d + j) % RING, 0:FB * P].rearrange("p (k n) -> p k n", k=FB)
                    pe.wait_ge(y_copied, 8 * q + j + 1 - 3 + Y_CREDIT + turn * RING)
                    for k in range(FB):
                        last = pe.matmul(ps[Y_BANKS[j]][:, t0:T], w[:, k, :], hT[:, k, t0:T],
                                         start=k == 0, stop=k == FB - 1)
                    last.then_inc(pieces_done, 1)
                over_pieces(pe, DOWN_PIECES, down)

            def proj(l):
                n0 = FIRST_PIECE["in", l]
                input_ready(l, 1, (0, 1))
                piece = None
                for n, (kind, j, c0, w, _) in enumerate(UNITS):
                    if j != piece:
                        landed(n0 + j)
                        piece = j
                    pw = IN_PIECES[j][1]
                    wv = ring[:, (n0 + j) % RING, 0:KC * pw].rearrange("p (k n) -> p k n", k=KC)
                    if n >= 4:
                        pe.wait_ge(proj_copied, NU * l + n - 3)
                    bank = ps[n % 4]
                    if kind == "fm":
                        base = 64 if w == 32 else 0
                        for k in range(KC):
                            last = pe.matmul(bank[base:base + w, :], wv[:, k, c0:c0 + w], uT[:, k, :],
                                             start=k == 0, stop=k == KC - 1)
                    else:
                        for k in range(KC):
                            last = pe.matmul(bank[:, 0:w], uT[:, k, kind * P:(kind + 1) * P],
                                             wv[:, k, c0:c0 + w], start=k == 0, stop=k == KC - 1)
                    last.then_inc(proj_ready, 1)
                    if n + 1 == NU or UNITS[n + 1][1] != j:
                        pe.drain().then_inc(pieces_done, 1)

            def mla_prep(l):
                pe.wait_ge(sem("c_squared"), 3 * (l + 1))
                for t in range(NT):
                    for m in range(2):
                        pe.matmul(ps[6][:, t:t + 1], csq[:, m, t * P:(t + 1) * P], ones[:, 0:1],
                                  start=m == 0, stop=m == 1)
                for t in range(NT):
                    last = pe.matmul(ps[6][:, 4 + t:5 + t], csq[:, 2, t * P:(t + 1) * P], ones[:, 0:1],
                                     start=True, stop=True)
                last.then_inc(sem("c_sums"), 1)
                pe.wait_ge(sem("c_rstd"), l + 1)
                for b, bank in ((0, ps[5]), (1, ps[7])):
                    for t in range(NT):
                        last = pe.matmul(bank[:, t * P:(t + 1) * P],
                                         rst[:, 4 * b + t:4 * b + t + 1].to_broadcast([P, P]),
                                         ident, start=True, stop=True)
                last.then_inc(sem("c_spread"), 1)
                pe.wait_ge(sem("c_normed"), l + 1)
                pe.wait_ge(mla_w_in, 32 * (l + 1))
                wq = mlaw[:, 0:768].rearrange("p (k n) -> p k n", k=2)
                for h in range(NH):
                    for k in range(2):
                        last = pe.matmul(ps[h][0:96, :], wq[:, k, h * 96:(h + 1) * 96], cT[:, k, :],
                                         start=k == 0, stop=k == 1)
                    last.then_inc(sem("mla_q"), 1)
                for h in range(NH):
                    pe.matmul(ps[4 + h][0:64, :], mlaw[:, 768 + h * P:768 + h * P + 64], cT[:, 2, :],
                              start=True, stop=True).then_inc(sem("mla_k"), 1)
                wv = mlaw[:, 768:1280].rearrange("p (h n) -> p h n", h=NH)[:, :, 64:128]
                pe.wait_ge(sem("mla_q_copied"), NH * (l + 1))
                for t in range(NT):
                    last = pe.matmul(ps[t // 2][:, (t % 2) * 256:(t % 2) * 256 + 256],
                                     cT[:, 2, t * P:(t + 1) * P], wv, start=True, stop=True)
                last.then_inc(sem("mla_v"), 1)
                rot = cst[64:96, C_ROT:C_ROT + 32]
                for h in range(NH):
                    last = pe.matmul(ps[2 + h // 2][64:96, (h % 2) * LAT:(h % 2 + 1) * LAT], rot,
                                     mqT[64:96, h, CTX:T], start=True, stop=True)
                last.then_inc(sem("q_turned"), 1)
                pe.wait_ge(sem("mla_k_copied"), NH * (l + 1))
                pe.matmul(ps[4][64:96, 0:LAT], rot, krT[64:96, CTX:T], start=True, stop=True
                          ).then_inc(sem("k_turned"), 1)

            def attention(l):
                units = att_units(l)
                u0 = ATT_BEFORE[l]
                pe.wait_ge(sem("bias_masked"), l + 1)
                pe.wait_ge(sem("mla_v_copied"), NT * (l + 1))

                def keys(t):
                    return 4 if t >= 2 else 2

                def scores(u):
                    mx, t, h = units[u]
                    if u >= 2:
                        pe.wait_ge(sem("att_exp"), u0 + u - 1)
                    n = keys(t) * P
                    bank = ps[u % 2]
                    if mx == 0:
                        q, k = mqT[0:96, h, t * P:(t + 1) * P], mkT[0:96, h, 0:n]
                    else:
                        at = slice(64 * (h % 2), 64 * (h % 2) + 64)
                        q, k = nqkT[at, h // 2, t * P:(t + 1) * P], nqkT[at, 2 + h // 2, 0:n]
                    biased = mx == 1 and t >= 2
                    last = pe.matmul(bank[:, 0:n], q, k, start=True, stop=not biased, skip_group_check=True)
                    if biased:
                        last = pe.matmul(bank[:, CTX:T], flip, natb[:, t - 2, h, :], start=False, stop=True,
                                         skip_group_check=True)
                    last.then_inc(sem("att_scores"), 1)

                def turn(u):
                    _, t, _ = units[u]
                    pe.wait_ge(sem("att_exp"), u0 + u + 1)
                    if u >= 2:
                        pe.wait_ge(sem("att_turned_copied"), u0 + u - 1)
                    for b in range(keys(t)):
                        last = pe.transpose(ps[2 + u % 2][:, b * P:(b + 1) * P],
                                            prob[:, u % 2, b * P:(b + 1) * P], ident)
                    last.then_inc(sem("att_turned"), 1)

                def weigh(u):
                    mx, t, h = units[u]
                    v = (mlav, natv)[mx]
                    pe.wait_ge(sem("att_turned_copied"), u0 + u + 1)
                    if u >= 2:
                        pe.wait_ge(sem("att_out"), u0 + u - 1)
                    for b in range(keys(t)):
                        last = pe.matmul(ps[4 + u % 2][:, 0:64], probT[:, u % 2, b * P:(b + 1) * P],
                                         v[:, b, h * 64:(h + 1) * 64], start=b == 0, stop=b == keys(t) - 1)
                    last.then_inc(sem("att_weighed"), 1)

                for u in range(len(units) + 2):
                    if u < len(units):
                        scores(u)
                    if 1 <= u <= len(units):
                        turn(u - 1)
                    if u >= 2:
                        weigh(u - 2)
                pe.wait_ge(sem("att_normed"), l + 1)
                for b in range(4):
                    for t in tiles_of(halves(l, True)):
                        last = pe.transpose(ps[b][:, t * P:(t + 1) * P],
                                            att_o[:, b // 2, t, (b % 2) * P:(b % 2 + 1) * P], ident)
                    last.then_inc(sem("att_feature_major"), 1)

            def scan_prep(l):
                pe.wait_ge(sem("qk_squared"), l + 1)
                for t in range(NT):
                    for b in range(4):
                        last = pe.matmul(ps[6][:, t * 8 + b * 2:t * 8 + b * 2 + 2],
                                         qksq[:, b, t * P:(t + 1) * P], cst[:, C_SEL:C_SEL + 2],
                                         start=True, stop=True)
                last.then_inc(sem("qk_sums"), 1)
                pe.wait_ge(sem("g_ready"), l + 1)
                g = gates[:, 5]
                for t in range(NT):
                    for d in range(2):
                        pe.matmul(ps[7][:, t * 16 + d * 8:t * 16 + d * 8 + 8], tri(d),
                                  g[:, t, d * 8:d * 8 + 8], start=True, stop=True)
                for t in range(NT):
                    last = pe.matmul(ps[7][:, 64 + t * 16:80 + t * 16], ones, g[:, t, :], start=True, stop=True)
                last.then_inc(sem("g_cumulated"), 1)
                pe.wait_ge(sem("qk_rstd"), l + 1)
                for b in range(4):
                    for t in range(NT):
                        for i in range(2):
                            c0 = t * 8 + b * 2 + i
                            last = pe.matmul(ps[b][64 * i:64 * i + 64, t * P:(t + 1) * P],
                                             rst[:, c0:c0 + 1].to_broadcast([P, 64]), ident,
                                             start=True, stop=True)
                    last.then_inc(sem("qk_spread"), 1)
                for n, b in enumerate((4, 5, 6, 7, 8, 9, 2, 3)):
                    if n == 6:
                        pe.wait_ge(sem("qk_normed"), 4 * (l + 1))
                    if n >= 2:
                        pe.wait_ge(sem("tm_copied"), 8 * l + n - 1)
                    for t in range(NT):
                        last = pe.transpose(ps[4 + n % 2][:, t * P:(t + 1) * P],
                                            convT[:, b, t * P:(t + 1) * P], ident)
                    last.then_inc(sem("tm_turned"), 1)

            def decays(bank, t, d, kind):
                last = pe.matmul(bank[:, :].rearrange("p (h n) -> p h n", h=NH), ident,
                                 negmask(d).unsqueeze(1).to_broadcast([P, NH, P]), start=True, stop=False,
                                 skip_group_check=True)
                for h in range(NH):
                    c0 = d * 8 + kind * 4 + h
                    last = pe.matmul(bank[:, h * P:(h + 1) * P],
                                     gates[:, 5, t, c0:c0 + 1].to_broadcast([P, P]), tri(d),
                                     start=False, stop=h == NH - 1, skip_group_check=True)
                return last

            def invert(l):
                for t in range(NT):
                    w0 = (l * NT + t) * 2
                    if t:
                        pe.wait_ge(sem("lt_ready"), w0)
                    for i, blk in enumerate((2, 0)):
                        for h in range(NH):
                            at = slice(64 * (h % 2), 64 * (h % 2) + 64)
                            last = pe.matmul(ps[h % 2][:, (2 * i + h // 2) * P:(2 * i + h // 2 + 1) * P],
                                             convT[at, 2 + h // 2, t * P:(t + 1) * P],
                                             convT[at, blk + h // 2, t * P:(t + 1) * P], start=True, stop=True)
                    last.then_inc(sem("kk_ready"), 1)
                    for d in range(2):
                        if t:
                            pe.wait_ge(sem("tu_done"), (w0 - 2) * N_LEVELS + 2 * (N_LEVELS - 1) + d + 1)
                        decays(ps[2 + d], t, d, 0).then_inc(sem("gr_ready"), 1)
                    for s in range(N_LEVELS):
                        c0 = w0 * N_LEVELS + 2 * s
                        c1 = w0 * NLV + 2 * (s - 1)
                        for d in range(2):
                            pe.wait_ge(sem("xt_ready"), c0 + d + 1)
                            if s:
                                pe.wait_ge(sem("tu_done"), c0 - 2 + d + 1)
                            for h in range(NH):
                                hs = slice(h * P, (h + 1) * P)
                                last = pe.matmul(ps[2 + d][:, hs], XT[:, d, hs],
                                                 Tm[:, d, hs] if s else ident, start=True, stop=True)
                            last.then_inc(sem("p1_ready"), 1)
                        if s == 0:
                            continue
                        for d in range(2):
                            pe.wait_ge(sem("p1_copied"), c1 + d + 1)
                            for h in range(NH):
                                hs = slice(h * P, (h + 1) * P)
                                if s < N_LEVELS - 1:
                                    pe.matmul(ps[4 + d][:, hs], UT[:, d, t, hs], P1[:, d, hs],
                                              start=True, stop=True)
                                last = pe.matmul(ps[6 + d][:, hs], P1[:, d, hs], UT[:, d, t, hs],
                                                 start=True, stop=True)
                            last.then_inc(sem("tu_ready"), 1)

            def scan(l):
                for n in range(NT):
                    k = l * NT + n
                    ts = [tile_of(d, n) for d in range(2)]
                    if n:
                        pe.wait_ge(sem("sg_ready"), k)
                        for bank, blk in ((ps[0], 2), (ps[1], 0)):
                            for d in range(2):
                                for i in range(2):
                                    last = pe.matmul(bank[:, (2 * d + i) * P:(2 * d + i + 1) * P],
                                                     convT[:, blk + i, ts[d] * P:(ts[d] + 1) * P],
                                                     S_g[:, 2 * d + i, :], start=True, stop=True)
                        last.then_inc(sem("ks_ready"), 1)
                    if n:
                        pe.wait_ge(sem("ss_ready"), k)
                    for d in range(2):
                        tk = slice(ts[d] * P, (ts[d] + 1) * P)
                        for g in range(2):
                            last = pe.matmul(ps[5][:, (2 * d + g) * P:(2 * d + g + 1) * P], convT[:, 8 + g, tk],
                                             convT[:, 10 + g, tk], start=True, stop=True)
                    last.then_inc(sem("bc_ready"), 1)
                    for d in range(2):
                        decays(ps[6 + d], ts[d], d, 1).then_inc(sem("sgr_ready"), 1)
                    pe.wait_ge(sem("r_ready"), k + 1)
                    for d in range(2):
                        for h in range(NH):
                            last = pe.matmul(ps[2][:, d * 256 + h * 64:d * 256 + h * 64 + 64],
                                             UT[:, d, ts[d], h * P:(h + 1) * P],
                                             r_g[:, d, h * 64:(h + 1) * 64], start=True, stop=True)
                    last.then_inc(sem("vn_solved"), 1)
                    pe.wait_ge(sem("sc_ready"), k + 1)
                    pe.wait_ge(sem("xd_ready"), k + 1)
                    for d in range(2):
                        for h in range(NH):
                            last = pe.matmul(ps[6][:, d * 256 + h * 64:d * 256 + h * 64 + 64],
                                             sc_s[:, d, h * P:(h + 1) * P], xdt[:, d, h * 64:(h + 1) * 64],
                                             start=True, stop=True)
                    for d in range(2):
                        for g in range(2):
                            o = slice(d * 256 + g * P, d * 256 + (g + 1) * P)
                            if n:
                                pe.matmul(ps[7][:, o], convT[:, 10 + g, ts[d] * P:(ts[d] + 1) * P],
                                          S_s[:, d, g * P:(g + 1) * P], start=True, stop=True)
                            last = pe.matmul(ps[5][:, o], b_tm[:, ts[d], g * P:(g + 1) * P],
                                             xdc[:, d, g * P:(g + 1) * P], start=True, stop=True)
                    last.then_inc(sem("ys_ready"), 1)
                    pe.wait_ge(sem("vn_ready"), k + 1)
                    pe.wait_ge(sem("kd_ready"), k + 1)
                    for d in range(2):
                        for h in range(NH):
                            hs = slice(h * 64, (h + 1) * 64)
                            pe.matmul(ps[3][:, d * 256 + h * 64:d * 256 + h * 64 + 64],
                                      AT[:, d, ts[d], h * P:(h + 1) * P], vn_g[:, d, hs], start=True, stop=True)
                            at = 64 * (h % 2)
                            last = pe.matmul(ps[4][at:at + 64, (2 * d + h // 2) * 64:(2 * d + h // 2 + 1) * 64],
                                             kd_g[:, d, hs], vn_g[:, d, hs], start=True, stop=True)
                    last.then_inc(sem("og_ready"), 1)

            def scan_out(l):
                pe.wait_ge(sem("scan_normed"), l + 1)
                for b, src in enumerate((o_tm, o_tm, y_tm, y_tm)):
                    for t in tiles_of(halves(l, True)):
                        last = pe.transpose(ps[b][:, t * P:(t + 1) * P],
                                            src[:, t, (b % 2) * P:(b % 2 + 1) * P], ident)
                    last.then_inc(sem("scan_feature_major"), 1)

            def out_proj(l, hs):
                t0 = HALF * hs[0]
                q = 3 * l + 1
                for j in range(OUT_PIECES):
                    n = FIRST_PIECE["out", l] + j
                    landed(n)
                    w = ring[:, n % RING, 0:4096].rearrange("p (k n) -> p k n", k=KC)
                    for b in range(4):
                        m = 4 * j + b
                        pe.wait_ge(y_copied, 8 * q + m + 1 - 3 + Y_CREDIT)
                        for k in range(KC):
                            last = pe.matmul(ps[Y_BANKS[m % 3]][:, t0:T], w[:, k, b * P:(b + 1) * P],
                                             uT[:, k, t0:T], start=k == 0, stop=k == KC - 1)
                        last.then_inc(y_mixed, 1)
                    pe.drain().then_inc(pieces_done, 1)

            def store():
                pe.wait_ge(x_ready, 8 * 3 * LAYERS)
                for t in range(2):
                    for i in range(2):
                        for m in range(4):
                            last = pe.transpose(ps[2 * t + i][:, m * P:(m + 1) * P],
                                                xT[:, 4 * i + m, CTX + t * P:CTX + (t + 1) * P], ident)
                        last.then_inc(sem("out_turned"), 1)

            setup()
            meet()
            for l in range(LAYERS):
                both, hs = halves(l, False), halves(l, True)
                mod(l)
                prenorm(l, 0, both)
                ffn(l, 0, both)
                postnorm(l, 0, both)
                prenorm(l, 1, both)
                proj(l)
                meet()
                mla_prep(l)
                attention(l)
                meet()
                scan_prep(l)
                meet()
                invert(l)
                meet()
                scan(l)
                scan_out(l)
                meet()
                out_proj(l, hs)
                postnorm(l, 1, hs)
                prenorm(l, 2, hs)
                ffn(l, 1, hs)
                postnorm(l, 2, hs)
            store()

        @block.scalar
        def _(act):
            meet = meeting(act)
            link = linked(act, sem("act_link"))
            A = nc.scalar.activation

            def setup():
                act.wait_ge(params_in, 16 * PARAM_DMAS)
                act.wait_ge(sem("const_set"), 1)
                act.wait_ge(setup_t, 1)
                A(prm[:, :, :].rearrange("p l n -> p (l n)"), ps[0][:, 0:LAYERS * 196], ACT.Copy
                  ).then_inc(setup_copied, 1)
                act.wait_ge(setup_t, 2)
                A(scT[:, :, :].rearrange("p k v -> p v k"), ps[1][:, 0:16].rearrange("p (v k) -> p v k", v=2),
                  ACT.Silu).then_inc(setup_copied, 1)
                for m in range(KC):
                    act.wait_ge(setup_t, 3 + m)
                    A(xT[:, m, :], ps[(2 + m) % 8][:, :], ACT.Copy).then_inc(setup_copied, 1)
                for l in range(LAYERS):
                    link(A(gpar[:, l, 16:32], gpar[:, l, 16:32], ACT.Exp))
                for n in range(Y_CREDIT):
                    A(small[:, 60 + n:61 + n], epsc[:, 0:1], ACT.Copy).then_inc(y_copied, 1)

            def norm(n, tiles):
                act.wait_ge(sums_ready, n + 1)
                a, b = tiles[0], tiles[-1] + 1
                A(std[:, a:b], ps[6][:, a:b], ACT.Sqrt, bias=epsc[:, 0:1], scale=1.0 / D).then_inc(rms_ready, 1)

            def prenorm(l, j, hs):
                t0 = HALF * hs[0]
                p = 3 * l + j
                for m in range(KC):
                    if p:
                        act.wait_ge(x_ready, 8 * (p - 1) + m + 1)
                    A(sq[:, m, t0:T], xT[:, m, t0:T], ACT.Square).then_inc(x_squared, 1)
                norm(6 * l + 2 * j, tiles_of(hs))
                if 0 in hs:
                    act.wait_ge(mod_ready, l + 1)
                    for m in range(KC):
                        act.wait_ge(x_scaled, 8 * p + m + 1)
                        A(uT[:, m, 0:CTX], uT[:, m, 0:CTX], ACT.Identity, scale=gpre[:, j, m, 0:1],
                          bias=modT[:, 3 * j * KC + m, 0:1]).then_inc(u_act, 1)

            def postnorm(l, j, hs):
                norm(6 * l + 2 * j + 1, tiles_of(hs))

            def ffn(l, f, hs):
                t0 = HALF * hs[0]
                u, d = FIRST_PIECE[f"up{f}", l], FIRST_PIECE[f"down{f}", l]
                i = 2 * l + f

                def up(turn, j):
                    for b in range(2):
                        if b == 0:
                            act.wait_ge(even_up, UP_PIECES * i + j + 1 + turn * RING)
                        else:
                            act.wait_ge(pieces_done, u + j + 1 + turn * RING)
                        act.wait_ge(gated, FB * i + 2 * j + b - 1 + GATE_CREDIT + turn * (2 * RING))
                        A(silu_t[:, b, t0:T], ps[2 * b][:, t0:T], ACT.Silu).then_inc(silu_done, 1)
                over_pieces(act, UP_PIECES, up)

                def down(turn, j):
                    act.wait_ge(pieces_done, d + j + 1 + turn * RING)
                    A(uTf[:, bass.ds(turn * (RING * T) + j * T + t0, T - t0)], ps[Y_BANKS[j]][:, t0:T],
                      ACT.Copy).then_inc(y_copied, 1)
                over_pieces(act, DOWN_PIECES, down)

            def proj(l):
                for n, (kind, j, c0, w, (to, b)) in enumerate(UNITS):
                    act.wait_ge(proj_ready, NU * l + n + 1)
                    bank = ps[n % 4]
                    scale = 1.0
                    if to == "cin":
                        dst, src = cin[:, b, :, 2:258], bank[:, :].rearrange("p (s n) -> p s n", s=2)
                    elif to == "krT":
                        dst, src = krT[64:96, :], bank[64:96, :]
                    elif to in ("cT", "nqkT"):
                        dst, src = {"cT": cT, "nqkT": nqkT}[to][:, b, :], bank[:, :]
                        scale = NAT_SCALE if to == "nqkT" and b < 2 else 1.0
                    else:
                        dst = {"zgG": zgG, "zgS": zgS, "dtr": dtr, "natv": natv}[to][:, b, :]
                        src = bank[:, 0:w]
                    A(dst, src, ACT.Copy, scale=scale).then_inc(proj_copied, 1)
                for b in range(12):
                    act.wait_ge(conv_done, 12 * l + b + 1)
                    bias = prm[:, l, 180 + b - 6:181 + b - 6] if b >= 6 else 0.0
                    A(convT[:, b, :], convT[:, b, :], ACT.Silu, bias=bias)
                A(zgG[:, :, 0:256], zgG[:, :, 0:256], ACT.Silu)
                A(zgS[:, :, :], zgS[:, :, :], ACT.Silu)

            def mla_prep(l):
                for b in range(3):
                    A(csq[:, b, :], cT[:, b, :], ACT.Square).then_inc(sem("c_squared"), 1)
                act.wait_ge(sem("c_sums"), l + 1)
                A(std[:, 0:4], ps[6][:, 0:4], ACT.Sqrt, bias=epsc[:, 0:1], scale=1.0 / 256)
                A(std[:, 4:8], ps[6][:, 4:8], ACT.Sqrt, bias=epsc[:, 0:1], scale=1.0 / 128
                  ).then_inc(sem("c_std"), 1)
                for h in range(NH):
                    act.wait_ge(sem("mla_q"), NH * l + h + 1)
                    A(mqT[0:96, h, :], ps[h][0:96, :], ACT.Copy, scale=MLA_SCALE).then_inc(sem("mla_q_copied"), 1)
                act.wait_ge(sem("mla_v"), l + 1)
                for t in range(NT):
                    A(mlav[:, t, :], ps[t // 2][:, (t % 2) * 256:(t % 2) * 256 + 256], ACT.Copy
                      ).then_inc(sem("mla_v_copied"), 1)

            def attention(l):
                units = att_units(l)
                u0 = ATT_BEFORE[l]
                for u, (mx, t, h) in enumerate(units):
                    n = (4 if t >= 2 else 2) * P
                    act.wait_ge(sem("att_max"), u0 + u + 1)
                    if u >= 2:
                        act.wait_ge(sem("att_turned"), u0 + u - 1)
                    if u >= 4:
                        act.wait_ge(sem("att_out"), u0 + u - 3)
                    A(prob[:, u % 2, 0:n], ps[u % 2][:, 0:n], ACT.Exp, bias=small[:, u % 4:u % 4 + 1],
                      accum_out=small[:, 8 + u % 4:9 + u % 4]).then_inc(sem("att_exp"), 1)
                act.wait_ge(sem("att_sums"), l + 1)
                A(std[:, 0:8], small[:, 24:32], ACT.Sqrt, bias=epsc[:, 0:1], scale=1.0 / 256
                  ).then_inc(sem("att_std"), 1)
                t0 = HALF * halves(l, True)[0]
                for b in range(4):
                    act.wait_ge(sem("att_feature_major"), 4 * l + b + 1)
                    A(uT[:, b, t0:T], ps[b][:, t0:T], ACT.Copy, scale=prm[:, l, 189 + b:190 + b])

            def scan_prep(l):
                A(qksq[:, :, :], convT[:, 0:4, :], ACT.Square).then_inc(sem("qk_squared"), 1)
                act.wait_ge(sem("gate_abs"), l + 1)
                A(gates[:, 2], gates[:, 1], ACT.Exp, scale=-1.0)
                A(gates[:, 7, :, 0:8], zgG[:, :, 256:264], ACT.Exp, scale=-1.0).then_inc(sem("gate_exp"), 1)
                act.wait_ge(sem("gate_w"), l + 1)
                A(gates[:, 4], gates[:, 3], ACT.Ln).then_inc(sem("gate_ln"), 1)
                act.wait_ge(sem("qk_sums"), l + 1)
                act.wait_ge(sem("gates_cumulated"), l + 1)
                A(gates[:, 2:5], gates[:, 8:11], ACT.Exp).then_inc(sem("decays_ready"), 1)
                A(std[:, 0:32], ps[6][:, 0:32], ACT.Sqrt, bias=epsc[:, 0:1]).then_inc(sem("qk_std"), 1)
                for n in range(8):
                    act.wait_ge(sem("tm_turned"), 8 * l + n + 1)
                    dst = (v_tm, v_tm, x_tm, x_tm, b_tm, b_tm, k_tm, k_tm)[n]
                    A(dst[:, :, (n % 2) * P:(n % 2 + 1) * P],
                      ps[4 + n % 2][:, :].rearrange("p (t n) -> p t n", t=NT), ACT.Copy
                      ).then_inc(sem("tm_copied"), 1)

            def exps(bank, dst, t, d, kind, s):
                for h in range(NH):
                    c0 = d * 8 + kind * 4 + h
                    last = A(dst[:, d, h * P:(h + 1) * P], bank[:, h * P:(h + 1) * P], ACT.Exp,
                             bias=gates[:, 1, t, c0:c0 + 1])
                last.then_inc(s, 1)

            def invert(l):
                for t in range(NT):
                    w0 = (l * NT + t) * 2
                    for d in range(2):
                        act.wait_ge(sem("gr_ready"), w0 + d + 1)
                        if t:
                            act.wait_ge(sem("lt_ready"), w0 - 2 + d + 1)
                        exps(ps[2 + d], dec, t, d, 0, sem("dec_ready"))
                    for s in range(1, N_LEVELS):
                        c0 = w0 * N_LEVELS + 2 * s
                        for d in range(2):
                            act.wait_ge(sem("p1_ready"), c0 + d + 1)
                            A(P1[:, d, :], ps[2 + d][:, :], ACT.Copy).then_inc(sem("p1_copied"), 1)

            def scan(l):
                for n in range(NT):
                    k = l * NT + n
                    for d in range(2):
                        act.wait_ge(sem("sgr_ready"), 2 * k + d + 1)
                        if n:
                            act.wait_ge(sem("sc_ready"), k)
                        exps(ps[6 + d], sdec, tile_of(d, n), d, 1, sem("sdec_ready"))
                act.wait_ge(sem("scan_sums"), l + 1)
                A(std[:, 0:16], small[:, 32:48], ACT.Sqrt, bias=epsc[:, 0:1], scale=1.0 / 64)
                A(std[:, 16:24], small[:, 48:56], ACT.Sqrt, bias=epsc[:, 0:1], scale=1.0 / 128
                  ).then_inc(sem("scan_std"), 1)
                t0 = HALF * halves(l, True)[0]
                for b in range(4):
                    act.wait_ge(sem("scan_feature_major"), 4 * l + b + 1)
                    at = (195, 195, 193, 194)[b]
                    A(uT[:, 4 + b, t0:T], ps[b][:, t0:T], ACT.Copy, scale=prm[:, l, at:at + 1])

            def out_proj(l, hs):
                t0 = HALF * hs[0]
                for m in range(KC):
                    act.wait_ge(y_mixed, 8 * l + m + 1)
                    A(view(m * T + t0, T - t0), ps[Y_BANKS[m % 3]][:, t0:T], ACT.Copy).then_inc(y_copied, 1)

            def store():
                for i in range(4):
                    act.wait_ge(sem("out_turned"), i + 1)
                    A(view(i * 512, 512), ps[i][:, :], ACT.Copy).then_inc(sem("out_copied"), 1)

            setup()
            meet()
            for l in range(LAYERS):
                both, hs = halves(l, False), halves(l, True)
                prenorm(l, 0, both)
                ffn(l, 0, both)
                postnorm(l, 0, both)
                prenorm(l, 1, both)
                proj(l)
                meet()
                mla_prep(l)
                attention(l)
                meet()
                scan_prep(l)
                meet()
                invert(l)
                meet()
                scan(l)
                meet()
                out_proj(l, hs)
                postnorm(l, 1, hs)
                prenorm(l, 2, hs)
                ffn(l, 1, hs)
                postnorm(l, 2, hs)
            store()

        @block.vector
        def _(dve):
            meet = meeting(dve)
            link = linked(dve, sem("dve_link"))
            V = nc.vector
            TT, STT, TS = V.tensor_tensor, V.scalar_tensor_tensor, V.tensor_scalar

            def wide(a, n):
                return a.unsqueeze(len(a.shape)).to_broadcast([*a.shape, n])

            def heads(a):
                return a.rearrange("p (h n) -> p h n", h=NH)

            def setup():
                V.memset(epsc[:, :], EPS).then_inc(sem("const_set"), 1)
                for n in range(GATE_CREDIT):
                    V.memset(small[:, 56 + n:57 + n], 0.0).then_inc(gated, 1)

            def neg_a():
                for l in range(LAYERS):
                    link(TS(gpar[:, l, 16:32], gpar[:, l, 16:32], -1.0, None, ALU.mult))

            def mod(l):
                dve.wait_ge(pieces_done, FIRST_PIECE["mod", l] + MOD_PIECES)
                pm = ps[7][:, 0:2 * NMOD * KC].rearrange("p (m v) -> p m v", v=2)
                link(TT(modT[:, :, :], pm, wide(prm[:, l, 0:72], 2), ALU.add))
                for j in range(3):
                    def part(i):
                        return modT[:, (3 * j + i) * KC:(3 * j + i + 1) * KC, :]
                    g = [wide(prm[:, l, 72 + (2 * j + i) * KC:72 + (2 * j + i + 1) * KC], 2) for i in range(2)]
                    STT(gpre[:, j], part(1), 1.0, g[0], ALU.add, ALU.mult)
                    last = STT(gpost[:, j], part(2), 1.0 if j == 1 else 0.5, g[1], ALU.mult, ALU.mult)
                link(last)
                V.memset(small[:, 58:59], 0.0).then_inc(mod_ready, 1)

            def norm(n, tiles):
                dve.wait_ge(rms_ready, n + 1)
                a, b = tiles[0], tiles[-1] + 1
                V.reciprocal(rst[:, a:b], std[:, a:b]).then_inc(rstd_ready, 1)
                dve.wait_ge(rms_spread, n + 1)

            def prenorm(l, j, hs):
                t0 = HALF * hs[0]
                p = 3 * l + j
                norm(6 * l + 2 * j, tiles_of(hs))
                for m in range(KC + 1):
                    if m < KC:
                        TT(uT[:, m, t0:T], xT[:, m, t0:T], ps[5][:, t0:T], ALU.mult).then_inc(x_scaled, 1)
                    if m:
                        dve.wait_ge(x_scaled, 8 * p + m)
                        b = m - 1
                        TS(uT[:, b, CTX:T], uT[:, b, CTX:T], gpre[:, j, b, 1:2],
                           modT[:, 3 * j * KC + b, 1:2], ALU.mult, ALU.add).then_inc(u_dve, 1)

            def y_block(q, m, at, more=0):
                dve.wait_ge(y_copied, 8 * q + m + 1 + Y_CREDIT + more)
                dve.wait_ge(y_summed, 9 * q + m + 1 + more)
                TT(ysq[:, at[1]:T], at[0], at[0], ALU.mult).then_inc(y_sq, 1)
                dve.wait_ge(y_sq, 8 * q + m + 1 + more)
                TT(yacc[:, at[1]:T], yacc[:, at[1]:T], ysq[:, at[1]:T], ALU.add).then_inc(y_summed, 1)

            def postnorm(l, j, hs, y):
                t0 = HALF * hs[0]
                q = 3 * l + j
                norm(6 * l + 2 * j + 1, tiles_of(hs))
                for m in range(KC + 1):
                    if m < KC:
                        TT(y(m), y(m), ps[5][:, t0:T], ALU.mult).then_inc(y_scaled, 1)
                    if m:
                        dve.wait_ge(y_scaled, 8 * q + m)
                        for h in hs:
                            o = slice(h * HALF, (h + 1) * HALF)
                            a = h * HALF - t0
                            last = STT(xT[:, m - 1, o], y(m - 1)[:, a:a + HALF], gpost[:, j, m - 1, h:h + 1],
                                       xT[:, m - 1, o], ALU.mult, ALU.add)
                        last.then_inc(x_ready, 1)

            def ffn(l, f, hs):
                t0 = HALF * hs[0]
                u = FIRST_PIECE[f"up{f}", l]
                i, q = 2 * l + f, 3 * l + 2 * f
                hf = view(0, FB * T)

                def up(turn, j):
                    for b in range(2):
                        if b == 1:
                            dve.wait_ge(pieces_done, u + j + 1 + turn * RING)
                        dve.wait_ge(silu_done, FB * i + 2 * j + b + 1 + turn * (2 * RING))
                        TT(hf[:, bass.ds(turn * (2 * RING * T) + (2 * j + b) * T + t0, T - t0)],
                           silu_t[:, b, t0:T], ps[2 * b + 1][:, t0:T], ALU.mult).then_inc(gated, 1)
                over_pieces(dve, UP_PIECES, up)
                V.memset(yacc[:, :], 0.0).then_inc(y_summed, 1)

                def down(turn, j):
                    y_block(q, j, (uTf[:, bass.ds(turn * (RING * T) + j * T + t0, T - t0)], t0), turn * RING)
                over_pieces(dve, DOWN_PIECES, down)
                postnorm(l, 2 * f, hs, lambda m: uT[:, m, t0:T])

            def conv(l):
                dve.wait_ge(pads_zero, l + 1)
                for b in range(12):
                    dve.wait_ge(proj_copied, NU * l + CIN_UNIT[b] + 1)
                    dst = convT[:, b, :].rearrange("p (s n) -> p s n", s=2)
                    w0 = 120 + b if b < 6 else 150 + b - 6
                    link(TS(dst, cin[:, b, :, 0:256], prm[:, l, w0:w0 + 1], None, ALU.mult))
                    for k in range(1, 5):
                        last = STT(dst, cin[:, b, :, k:k + 256], prm[:, l, w0 + 6 * k:w0 + 6 * k + 1], dst,
                                   ALU.mult, ALU.add)
                        if k < 4:
                            link(last)
                    last.then_inc(conv_done, 1)

            def mla_prep(l):
                dve.wait_ge(sem("c_std"), l + 1)
                V.reciprocal(rst[:, 0:8], std[:, 0:8]).then_inc(sem("c_rstd"), 1)
                dve.wait_ge(sem("c_spread"), l + 1)
                for b in range(3):
                    last = STT(cT[:, b, :], cT[:, b, :], prm[:, l, 186 + b:187 + b], ps[5 if b < 2 else 7][:, :],
                               ALU.mult, ALU.mult)
                last.then_inc(sem("c_normed"), 1)
                for h in range(NH):
                    dve.wait_ge(sem("mla_k"), NH * l + h + 1)
                    V.tensor_copy(mkT[0:64, h, :], ps[4 + h][0:64, :]).then_inc(sem("mla_k_copied"), 1)
                lo = slice(64, 96)
                cos, sin = cst[lo, C_COS:C_COS + LAT], cst[lo, C_SIN:C_SIN + LAT]
                rt = rope_t[lo]
                dve.wait_ge(sem("q_turned"), l + 1)
                for i in range(2):
                    TT(rt[:, 2 * i:2 * i + 2, :], ps[2 + i][lo, :].rearrange("p (h n) -> p h n", h=2),
                       sin.unsqueeze(1).to_broadcast([32, 2, LAT]), ALU.mult)
                q = mqT[lo, :, CTX:T]
                link(TT(q, q, cos.unsqueeze(1).to_broadcast([32, NH, LAT]), ALU.mult))
                link(TT(q, q, rt, ALU.add))
                dve.wait_ge(sem("k_turned"), l + 1)
                TT(rt[:, 0, :], ps[4][lo, 0:LAT], sin, ALU.mult)
                kr = krT[lo, CTX:T]
                link(TT(kr, kr, cos, ALU.mult))
                link(TT(kr, kr, rt[:, 0, :], ALU.add))
                link(V.tensor_copy(mkT[lo, :, :], krT[lo, :].unsqueeze(1).to_broadcast([32, NH, T])))
                dve.wait_ge(nat_bias_in, 256 * (l + 1))
                nb = natb[:, :, :, :].rearrange("p t h n -> p (t h n)").rearrange("p (r n) -> p r n", n=RW)
                mask = cst[:, C_NATM:C_NATM + RW].unsqueeze(1).to_broadcast([P, 2 * NH * ROWS, RW])
                TT(nb, nb, mask, ALU.add).then_inc(sem("bias_masked"), 1)

            def attention(l):
                units = att_units(l)
                u0 = ATT_BEFORE[l]
                N = len(units)

                def top(u):
                    _, t, _ = units[u]
                    n = (4 if t >= 2 else 2) * P
                    dve.wait_ge(sem("att_scores"), u0 + u + 1)
                    V.tensor_reduce(small[:, u % 4:u % 4 + 1], ps[u % 2][:, 0:n], AX, ALU.max, negate=True
                                    ).then_inc(sem("att_max"), 1)

                def copy(u):
                    _, t, _ = units[u]
                    n = (4 if t >= 2 else 2) * P
                    dve.wait_ge(sem("att_turned"), u0 + u + 1)
                    if u >= 2:
                        dve.wait_ge(sem("att_weighed"), u0 + u - 1)
                    V.tensor_copy(probT[:, u % 2, 0:n], ps[2 + u % 2][:, 0:n]).then_inc(sem("att_turned_copied"), 1)
                    link(V.reciprocal(small[:, 12 + u % 4:13 + u % 4], small[:, 8 + u % 4:9 + u % 4]))

                def scale(u):
                    mx, t, h = units[u]
                    dve.wait_ge(sem("att_weighed"), u0 + u + 1)
                    TS(att_o[:, mx, t, h * 64:(h + 1) * 64], ps[4 + u % 2][:, 0:64],
                       small[:, 12 + u % 4:13 + u % 4], None, ALU.mult).then_inc(sem("att_out"), 1)

                for u in range(N + 2):
                    if u < N:
                        top(u)
                    if 1 <= u <= N:
                        copy(u - 1)
                    if u >= 2:
                        scale(u - 2)
                ts = tiles_of(halves(l, True))
                a, n = ts[0], len(ts)
                dve.wait_ge(sem("att_out"), u0 + N)
                o = att_o[:, :, a:a + n, :]
                if n < NT:
                    link(V.memset(small[:, 24:32], 1.0))
                for mx in range(2):
                    last = TT(att_sq[:, mx, a:a + n, :], o[:, mx], o[:, mx], ALU.mult)
                link(last)
                sums = small[:, 24:32].rearrange("p (m t) -> p m t", m=2)[:, :, a:a + n]
                V.tensor_reduce(sums, att_sq[:, :, a:a + n, :], AX, ALU.add).then_inc(sem("att_sums"), 1)
                dve.wait_ge(sem("att_std"), l + 1)
                link(V.reciprocal(rst[:, 0:8], std[:, 0:8]))
                r = rst[:, 0:8].rearrange("p (m t) -> p m t", m=2)
                for mx in range(2):
                    last = TT(o[:, mx], o[:, mx], wide(r[:, mx, a:a + n], 256), ALU.mult)
                last.then_inc(sem("att_normed"), 1)

            def scan_prep(l):
                G = [gates[:, i] for i in range(12)]

                def per_dir(a, w):
                    return a.rearrange("p t (d k h) -> p t d k h", d=2, k=2)[:, :, :, w, :]
                for w, raw in enumerate((zgG[:, :, 264:272], dtr[:, :, :])):
                    for d in range(2):
                        bias = gpar[:, l, d * 8 + w * 4:d * 8 + w * 4 + 4].unsqueeze(1).to_broadcast([P, NT, 4])
                        last = TT(G[0][:, :, d * 8 + w * 4:d * 8 + w * 4 + 4], raw[:, :, d * 4:d * 4 + 4], bias,
                                  ALU.add)
                link(last)
                STT(G[1], G[0], -1.0, G[0], ALU.mult, ALU.max).then_inc(sem("gate_abs"), 1)
                dve.wait_ge(sem("gate_exp"), l + 1)
                link(TS(G[3], G[2], 1.0, None, ALU.add))
                V.memset(small[:, 59:60], 0.0).then_inc(sem("gate_w"), 1)
                link(TS(G[5], G[3], -1.0, None, ALU.add))
                link(TT(G[5], G[2], G[5], ALU.subtract))
                link(V.reciprocal(G[6], G[3]))
                link(TT(G[5], G[5], G[6], ALU.mult))
                link(STT(G[5], G[0], 0.0, G[5], ALU.max, ALU.add))
                dve.wait_ge(sem("gate_ln"), l + 1)
                link(TT(G[6], G[5], G[4], ALU.add))
                TT(G[5], G[6], gpar[:, l, 16:32].unsqueeze(1).to_broadcast([P, NT, 16]), ALU.mult
                   ).then_inc(sem("g_ready"), 1)
                link(TS(G[7][:, :, 0:8], G[7][:, :, 0:8], 1.0, None, ALU.add))
                link(V.reciprocal(G[7][:, :, 0:8], G[7][:, :, 0:8]))
                dve.wait_ge(sem("g_cumulated"), l + 1)
                cum = ps[7][:, 0:64].rearrange("p (t c) -> p t c", t=NT)
                tot = ps[7][:, 64:128].rearrange("p (t c) -> p t c", t=NT)
                link(V.tensor_copy(G[8], cum))
                TS(G[1], cum, -1.0, None, ALU.mult)
                V.tensor_copy(G[10], tot)
                link(TT(G[9], tot, G[8], ALU.subtract))
                V.memset(small[:, 59:60], 0.0).then_inc(sem("gates_cumulated"), 1)
                dve.wait_ge(sem("qk_std"), l + 1)
                link(V.reciprocal(rst[:, 0:32], std[:, 0:32]))
                rq = rst[:, 0:32].rearrange("p (t c) -> p t c", t=NT)[:, :, 0:4]
                TS(rq, rq, GDN_SCALE, None, ALU.mult).then_inc(sem("qk_rstd"), 1)
                for b in range(4):
                    dve.wait_ge(sem("qk_spread"), 4 * l + b + 1)
                    TT(convT[:, b, :], convT[:, b, :], ps[b][:, :], ALU.mult).then_inc(sem("qk_normed"), 1)

            def invert(l):
                for t in range(NT):
                    w0 = (l * NT + t) * 2
                    dve.wait_ge(sem("kk_ready"), l * NT + t + 1)
                    for d in range(2):
                        dve.wait_ge(sem("dec_ready"), w0 + d + 1)
                        if t:
                            dve.wait_ge(sem("xt_ready"), (w0 - 2) * N_LEVELS + 2 * (N_LEVELS - 1) + d + 1)
                        def parity(a, par):
                            return a.rearrange("p (i r n) -> p r i n", r=2, n=P)[:, par]
                        for par in range(2):
                            TT(parity(AT[:, d, t, :], par), parity(dec[:, d, :], par),
                               ps[par][:, 256:512].rearrange("p (i n) -> p i n", i=2), ALU.mult)
                        beta = gates[:, 7, t, d * 4:d * 4 + 4]
                        link(TT(heads(LT[:, d, :]), heads(dec[:, d, :]), wide(beta, P), ALU.mult))
                        for par in range(2):
                            last = TT(parity(LT[:, d, :], par), parity(LT[:, d, :], par),
                                      ps[par][:, 0:256].rearrange("p (i n) -> p i n", i=2), ALU.mult)
                        last.then_inc(sem("lt_ready"), 1)
                    for s in range(N_LEVELS):
                        c0 = w0 * N_LEVELS + 2 * s
                        c1 = w0 * NLV + 2 * (s - 1)
                        for d in range(2):
                            if s == 0:
                                eye = ident.unsqueeze(1).to_broadcast([P, NH, P])
                                dve.wait_ge(sem("p1_ready"), c0 + d + 1)
                                TT(heads(Tm[:, d, :]), eye, heads(ps[2 + d][:, :]), ALU.subtract)
                                TT(heads(UT[:, d, t, :]), eye, heads(XT[:, d, :]), ALU.subtract
                                   ).then_inc(sem("tu_done"), 1)
                                continue
                            dve.wait_ge(sem("tu_ready"), c1 + d + 1)
                            if s < N_LEVELS - 1:
                                TT(Tm[:, d, :], Tm[:, d, :], ps[4 + d][:, :], ALU.subtract)
                            TT(UT[:, d, t, :], UT[:, d, t, :], ps[6 + d][:, :], ALU.subtract
                               ).then_inc(sem("tu_done"), 1)

            def scan(l):
                gl = std[:, 32:48].rearrange("p (t d h) -> p t d h", t=NT, d=2)
                link(V.memset(S_g[:, :, :], 0.0))
                for par in range(2):
                    at = slice(64 * par, 64 * par + 64)
                    for n in range(NT):
                        for d in range(2):
                            src = gates[at, 4, tile_of(d, n), d * 8:d * 8 + 4].rearrange("p (h r) -> p h r", r=2)
                            last = V.tensor_copy(gl[at, n, d, :], src[:, :, par])
                link(last)
                for n in range(NT):
                    k = l * NT + n
                    ts = [tile_of(d, n) for d in range(2)]

                    def gate(i, d, kind):
                        return gates[:, i, ts[d], d * 8 + kind * 4:d * 8 + kind * 4 + 4]
                    if n:
                        dve.wait_ge(sem("ks_ready"), l * (NT - 1) + n)
                        for d in range(2):
                            last = TT(heads(tmp_g[:, d, :]), heads(ps[0][:, d * 256:d * 256 + 256]),
                                      wide(gate(2, d, 0), 64), ALU.mult)
                        link(last)
                    for d in range(2):
                        if n:
                            last = TT(r_g[:, d, :], v_tm[:, ts[d], :], tmp_g[:, d, :], ALU.subtract)
                        else:
                            last = V.tensor_copy(r_g[:, d, :], v_tm[:, ts[d], :])
                    last.then_inc(sem("r_ready"), 1)
                    dve.wait_ge(sem("bc_ready"), k + 1)
                    for d in range(2):
                        dve.wait_ge(sem("sdec_ready"), 2 * k + d + 1)
                        bc = ps[5][:, d * 256:(d + 1) * 256].rearrange("p (g n) -> p g n", g=2)
                        last = TT(sc_s[:, d, :].rearrange("p (g r n) -> p g r n", g=2, r=2),
                                  sdec[:, d, :].rearrange("p (g r n) -> p g r n", g=2, r=2),
                                  bc.unsqueeze(2).to_broadcast([P, 2, 2, P]), ALU.mult)
                    last.then_inc(sem("sc_ready"), 1)
                    dve.wait_ge(sem("vn_solved"), k + 1)
                    for d in range(2):
                        last = TT(heads(vn_g[:, d, :]), heads(ps[2][:, d * 256:d * 256 + 256]),
                                  wide(gates[:, 7, ts[d], d * 4:d * 4 + 4], 64), ALU.mult)
                    last.then_inc(sem("vn_ready"), 1)
                    dve.wait_ge(sem("ys_ready"), k + 1)
                    st = ps[5][:, :].rearrange("p (d n) -> p d n", d=2)
                    if n:
                        for d in range(2):
                            last = TT(heads(S_s[:, d, :]), heads(S_s[:, d, :]), wide(gate(4, d, 1), 64), ALU.mult)
                        link(last)
                        link(TT(S_s[:, :, :], S_s[:, :, :], st, ALU.add))
                    else:
                        link(V.tensor_copy(S_s[:, :, :], st))
                    add_out(n, ts, y_tm, ps[7], ps[6], tmp_s, [gate(2, d, 1) for d in range(2)], sem("ss_ready"))
                    dve.wait_ge(sem("og_ready"), k + 1)
                    sg = ps[4][:, 0:256].rearrange("p (d n) -> p d n", d=4)
                    own = [(S_g[64 * r:64 * r + 64, :, 64 * r:64 * r + 64], slice(64 * r, 64 * r + 64))
                           for r in range(2)]
                    if n:
                        for s_own, at in own:
                            last = TT(s_own, s_own, wide(std[at, 32 + 4 * n:36 + 4 * n], 64), ALU.mult)
                        link(last)
                        for s_own, at in own:
                            last = TT(s_own, s_own, sg[at], ALU.add)
                    else:
                        for s_own, at in own:
                            last = V.tensor_copy(s_own, sg[at])
                    add_out(n, ts, o_tm, ps[1], ps[3], tmp_g, [gate(2, d, 0) for d in range(2)], sem("sg_ready"))
                xd = fin_sq[:, 1, :, :]
                link(TT(xd.rearrange("p t (h n) -> p t h n", h=NH),
                        x_tm[:, :, :].rearrange("p t (h n) -> p t h n", h=NH),
                        wide(gpar[:, l, 32:36], 64).unsqueeze(1).to_broadcast([P, NT, NH, 64]), ALU.mult))
                link(TT(y_tm[:, :, :], y_tm[:, :, :], xd, ALU.add))
                link(TT(y_tm[:, :, :], y_tm[:, :, :], zgS[:, :, :], ALU.mult))
                TT(fin_sq[:, 0, :, :], o_tm[:, :, :], o_tm[:, :, :], ALU.mult)
                link(TT(fin_sq[:, 1, :, :], y_tm[:, :, :], y_tm[:, :, :], ALU.mult))
                V.tensor_reduce(small[:, 32:48].rearrange("p (t h) -> p t h", t=NT),
                                fin_sq[:, 0, :, :].rearrange("p t (h n) -> p t h n", h=NH), AX, ALU.add)
                V.tensor_reduce(small[:, 48:56].rearrange("p (t g) -> p t g", t=NT),
                                fin_sq[:, 1, :, :].rearrange("p t (g n) -> p t g n", g=2), AX, ALU.add
                                ).then_inc(sem("scan_sums"), 1)
                dve.wait_ge(sem("scan_std"), l + 1)
                link(V.reciprocal(rst[:, 0:24], std[:, 0:24]))
                o4 = o_tm[:, :, :].rearrange("p t (h n) -> p t h n", h=NH)
                link(TT(o4, o4, wide(rst[:, 0:16].rearrange("p (t h) -> p t h", t=NT), 64), ALU.mult))
                TT(o_tm[:, :, :], o_tm[:, :, :], zgG[:, :, 0:256], ALU.mult)
                y4 = y_tm[:, :, :].rearrange("p t (g n) -> p t g n", g=2)
                TT(y4, y4, wide(rst[:, 16:24].rearrange("p (t g) -> p t g", t=NT), P), ALU.mult
                   ).then_inc(sem("scan_normed"), 1)

            def add_out(n, ts, out_tm, from_state, within, tmp, egc, done):
                for d in range(2):
                    o = slice(d * 256, d * 256 + 256)
                    first = n % 2 == 0
                    dst = out_tm[:, ts[d], :]
                    if n:
                        link(TT(heads(tmp[:, d, :]), heads(from_state[:, o]), wide(egc[d], 64), ALU.mult))
                        if first:
                            last = TT(dst, tmp[:, d, :], within[:, o], ALU.add)
                        else:
                            link(TT(tmp[:, d, :], tmp[:, d, :], within[:, o], ALU.add))
                            last = TT(dst, dst, tmp[:, d, :], ALU.add)
                    else:
                        last = V.tensor_copy(dst, within[:, o])
                last.then_inc(done, 1)

            def out_proj(l, hs):
                t0 = HALF * hs[0]
                q = 3 * l + 1
                V.memset(yacc[:, :], 0.0).then_inc(y_summed, 1)
                for m in range(KC):
                    y_block(q, m, (view(m * T + t0, T - t0), t0))
                postnorm(l, 1, hs, lambda m: view(m * T + t0, T - t0))

            setup()
            meet()
            neg_a()
            for l in range(LAYERS):
                both, hs = halves(l, False), halves(l, True)
                mod(l)
                prenorm(l, 0, both)
                ffn(l, 0, both)
                prenorm(l, 1, both)
                conv(l)
                meet()
                mla_prep(l)
                attention(l)
                meet()
                scan_prep(l)
                meet()
                invert(l)
                meet()
                scan(l)
                meet()
                out_proj(l, hs)
                prenorm(l, 2, hs)
                ffn(l, 1, hs)

        @block.gpsimd
        def _(pool):
            meet = meeting(pool)
            G = nc.gpsimd

            def wide(a, n):
                return a.unsqueeze(len(a.shape)).to_broadcast([*a.shape, n])

            def heads(a):
                return a.rearrange("p (h n) -> p h n", h=NH)

            meet()
            for l in range(LAYERS):
                pool.wait_ge(u_dve, 8 * (3 * l + 2))
                G.memset(cin[:, :, :, 0:2], 0.0)
                G.memset(cin[:, :, :, 258:260], 0.0).then_inc(pads_zero, 1)
                meet()
                meet()
                meet()
                for t in range(NT):
                    w0 = (l * NT + t) * 2
                    for s in range(N_LEVELS):
                        c0 = w0 * N_LEVELS + 2 * s
                        for d in range(2):
                            if s == 0:
                                pool.wait_ge(sem("lt_ready"), w0 + d + 1)
                                if t:
                                    pool.wait_ge(sem("p1_ready"), c0 - 2 + d + 1)
                            else:
                                pool.wait_ge(sem("p1_ready"), c0 - 2 + d + 1)
                                if s == 1:
                                    pool.wait_ge(sem("tu_done"), c0 - 2 + d + 1)
                            at = C_LEV + (d * N_LEVELS + s) * P
                            G.tensor_tensor(heads(XT[:, d, :]), heads(LT[:, d, :]),
                                            cst[:, at:at + P].unsqueeze(1).to_broadcast([P, NH, P]), ALU.mult
                                            ).then_inc(sem("xt_ready"), 1)
                meet()
                for n in range(NT):
                    k = l * NT + n
                    if n:
                        pool.wait_ge(sem("ys_ready"), k)
                    for d in range(2):
                        t = tile_of(d, n)
                        G.tensor_tensor(heads(xdt[:, d, :]), heads(x_tm[:, t, :]),
                                        wide(gates[:, 6, t, d * 8 + 4:d * 8 + 8], 64), ALU.mult
                                        ).then_inc(sem("xdt_ready"), 1)
                        pool.wait_ge(sem("xdt_ready"), 2 * k + d + 1)
                        last = G.tensor_tensor(heads(xdc[:, d, :]), heads(xdt[:, d, :]),
                                               wide(gates[:, 3, t, d * 8 + 4:d * 8 + 8], 64), ALU.mult)
                    last.then_inc(sem("xd_ready"), 1)
                    if n:
                        pool.wait_ge(sem("og_ready"), k)
                    for d in range(2):
                        t = tile_of(d, n)
                        last = G.tensor_tensor(heads(kd_g[:, d, :]), heads(k_tm[:, t, :]),
                                               wide(gates[:, 3, t, d * 8:d * 8 + 4], 64), ALU.mult)
                    last.then_inc(sem("kd_ready"), 1)
                meet()


_INS = ['x', 'c', 'ctx', 'c_ctx', 'w_mod', 'b_mod', 'norm_g', 'ffn1_w1', 'ffn1_w3', 'ffn1_w2',
        'ffn2_w1', 'ffn2_w3', 'ffn2_w2', 'w_in', 'w_out', 'mla_gq', 'mla_gkv', 'mla_wuq', 'mla_wukv',
        'mla_gout', 'nat_rpb', 'nat_gout', 'gdn_conv_w', 'gdn_a_log', 'gdn_dt_bias', 'gdn_gnorm',
        'ssm_conv_w', 'ssm_conv_b', 'ssm_a_log', 'ssm_dt_bias', 'ssm_d', 'ssm_gnorm']


def kernel(**inputs):
    import concourse.bacc as _bacc
    from concourse.bass_utils import run_bass_kernel_spmd as _run

    nc = _bacc.Bacc("TRN2", target_bir_lowering=False, num_devices=1)
    arrays, args = {}, {}
    for name in _INS:
        a = np.ascontiguousarray(inputs[name])
        arrays[f"in_{name}_dram"] = a
        args[name] = nc.dram_tensor(f"in_{name}_dram", a.shape, mybir.dt.from_np(a.dtype),
                                    kind="ExternalInput").ap()
    consts = constants(grid_w=64, window=16, theta=10000.0, rope=32, lat=inputs['x'].shape[1])
    arrays["consts_dram"] = consts
    c = nc.dram_tensor("consts_dram", consts.shape, F32, kind="ExternalInput").ap()
    out = nc.dram_tensor("out_dram", inputs['x'].shape, F32, kind="ExternalOutput").ap()
    trunk(nc, out, c, **args)
    r = _run(nc, [arrays], core_ids=[0])
    return r.results[0]["out_dram"]
```
